# Optimizing a Trainium2 kernel written in Bass

```python
import jax, jax.numpy as jnp
from jax import lax
import numpy as np

D_MODEL = 1024
BATCH = 1
SEQ = 256
DEPTH = 1

MLA_HEADS = 8
QK_NOPE = 64
QK_ROPE = 32
QK_HEAD = QK_NOPE + QK_ROPE
V_HEAD = 64
Q_LORA = 256
KV_LORA = 128
ROPE_THETA = 10000.0
Q_BLOCK = 128
CONV_GROUPS = 8
CONV_WIDTH = 512
CONV_K = 3
N_EXPERTS = 32
TOP_K = 4
D_FF = D_MODEL
SWIGLU_LIMIT = 7.0
SWIGLU_ALPHA = 1.702
EXPERT_BLOCK = 256
EPS = 1e-6
IN_SIZES = (Q_LORA, KV_LORA, QK_ROPE, CONV_WIDTH, CONV_WIDTH, CONV_WIDTH, D_MODEL, D_MODEL)
IN_COLS = sum(IN_SIZES)
IN_SPLITS = tuple(int(s) for s in np.cumsum(IN_SIZES)[:-1])

kernel_name = 'hybrid_mla_shortconv_moe_encoder'

def rms_norm(x, g):
    xf = x.astype(jnp.float32)
    y = xf * lax.rsqrt(jnp.mean(xf * xf, axis=-1, keepdims=True) + EPS)
    return (y * g.astype(jnp.float32)).astype(x.dtype)

def rope_tables(positions, dtype):
    inv_freq = ROPE_THETA ** (-jnp.arange(0, QK_ROPE, 2, dtype=jnp.float32) / QK_ROPE)
    ang = positions.astype(jnp.float32)[..., None] * inv_freq
    return jnp.cos(ang)[:, :, None, :].astype(dtype), jnp.sin(ang)[:, :, None, :].astype(dtype)

def apply_rope(t, cos, sin):
    t1, t2 = t[..., :QK_ROPE // 2], t[..., QK_ROPE // 2:]
    return jnp.concatenate([t1 * cos - t2 * sin, t1 * sin + t2 * cos], axis=-1)

def dense_attention(q, k, v):
    B, S, H, _ = q.shape
    nb = S // Q_BLOCK
    qb = q.reshape(B, nb, Q_BLOCK, H, QK_HEAD).transpose(1, 0, 3, 2, 4)
    kt = k.transpose(0, 2, 1, 3)
    vt = v.transpose(0, 2, 1, 3)
    scale = QK_HEAD ** -0.5

    def one_block(q_blk):
        s = jnp.einsum('bhqd,bhkd->bhqk', q_blk, kt, preferred_element_type=jnp.float32) * scale
        p = jax.nn.softmax(s, axis=-1)
        return jnp.einsum('bhqk,bhkd->bhqd', p.astype(vt.dtype), vt)

    o = lax.map(one_block, qb)
    return o.transpose(1, 0, 3, 2, 4).reshape(B, S, H * V_HEAD)

def mla_branch(c_q, c_kv, k_rope, cos, sin, q_a_g, kv_a_g, w_uq, w_ukv, q_g, k_g, w_o_mla):
    B, S, _ = c_q.shape
    q = (rms_norm(c_q, q_a_g) @ w_uq).reshape(B, S, MLA_HEADS, QK_HEAD)
    kv = (rms_norm(c_kv, kv_a_g) @ w_ukv).reshape(B, S, MLA_HEADS, QK_NOPE + V_HEAD)
    k_nope, v = kv[..., :QK_NOPE], kv[..., QK_NOPE:]
    k_r = jnp.broadcast_to(k_rope[:, :, None, :], (B, S, MLA_HEADS, QK_ROPE))
    k = jnp.concatenate([k_nope, k_r], axis=-1)
    q = rms_norm(q, q_g)
    k = rms_norm(k, k_g)
    q = jnp.concatenate([q[..., :QK_NOPE], apply_rope(q[..., QK_NOPE:], cos, sin)], axis=-1)
    k = jnp.concatenate([k[..., :QK_NOPE], apply_rope(k[..., QK_NOPE:], cos, sin)], axis=-1)
    return dense_attention(q, k, v) @ w_o_mla

def short_conv_branch(u, c_gate, b_gate, conv_w, w_o_conv):
    cu = c_gate * u
    p = jnp.pad(cu, ((0, 0), (1, 1), (0, 0)))
    y = conv_w[0] * p[:, :-2] + conv_w[1] * p[:, 1:-1] + conv_w[2] * p[:, 2:]
    return (b_gate * y) @ w_o_conv

def moe(h, router_w, router_b, w1, b1, w2, b2):
    B, S, D = h.shape
    n_tok = B * S
    hf = h.reshape(n_tok, D)
    logits = (hf @ router_w + router_b).astype(jnp.float32)
    top_v, top_i = lax.top_k(logits, TOP_K)
    top_w = jax.nn.softmax(top_v, axis=-1).astype(h.dtype)

    nk = n_tok * TOP_K
    e_flat = top_i.reshape(nk)
    w_flat = top_w.reshape(nk)
    tok_flat = jnp.arange(nk, dtype=jnp.int32) // TOP_K
    order = jnp.argsort(e_flat)
    e_sorted = e_flat[order]
    counts = jnp.bincount(e_flat, length=N_EXPERTS)
    group_start = jnp.cumsum(counts) - counts
    padded = (counts + EXPERT_BLOCK - 1) // EXPERT_BLOCK * EXPERT_BLOCK
    pad_end = jnp.cumsum(padded)
    pad_start = pad_end - padded
    rank = jnp.arange(nk, dtype=jnp.int32) - group_start[e_sorted]
    dest = pad_start[e_sorted] + rank
    n_blocks = (nk + N_EXPERTS * (EXPERT_BLOCK - 1) + EXPERT_BLOCK - 1) // EXPERT_BLOCK
    rows = n_blocks * EXPERT_BLOCK
    row_tok = jnp.zeros((rows,), jnp.int32).at[dest].set(tok_flat[order])
    row_w = jnp.zeros((rows,), h.dtype).at[dest].set(w_flat[order])
    block_exp = jnp.clip(jnp.searchsorted(pad_end, jnp.arange(n_blocks, dtype=jnp.int32) * EXPERT_BLOCK,
                                          side='right'), 0, N_EXPERTS - 1)
    xs = hf[row_tok].reshape(n_blocks, EXPERT_BLOCK, D)

    def expert_block(args):
        xb, e = args
        hm = xb @ w1[e] + b1[e]
        gate, up = hm[:, :D_FF], hm[:, D_FF:]
        gate = jnp.minimum(gate, SWIGLU_LIMIT)
        up = jnp.clip(up, -SWIGLU_LIMIT, SWIGLU_LIMIT)
        glu = gate * jax.nn.sigmoid(SWIGLU_ALPHA * gate)
        return ((up + 1.0) * glu) @ w2[e] + b2[e]

    ys = lax.map(expert_block, (xs, block_exp)).reshape(rows, D) * row_w[:, None]
    out = jax.ops.segment_sum(ys, row_tok, num_segments=n_tok)
    return out.reshape(B, S, D)

def setup_inputs(seed: int = 0) -> dict:
    key = jax.random.key(seed)
    ks = jax.random.split(key, 24)
    L = DEPTH

    def nrm(k, shape, fan_in):
        return jax.random.normal(k, shape, jnp.float32) * fan_in ** -0.5

    def gain(k, n):
        return 1.0 + 0.02 * jax.random.normal(k, (L, n), jnp.float32)

    x = jax.random.normal(ks[0], (BATCH, SEQ, D_MODEL), jnp.float32)
    offs = jax.random.randint(ks[1], (BATCH, 1), 0, 1024, dtype=jnp.int32)
    positions = jnp.arange(SEQ, dtype=jnp.int32)[None, :] + offs
    return {
        'x': x,
        'positions': positions,
        'norm1_g': gain(ks[2], D_MODEL),
        'w_in': nrm(ks[3], (L, D_MODEL, IN_COLS), D_MODEL),
        'q_a_norm_g': gain(ks[4], Q_LORA),
        'kv_a_norm_g': gain(ks[5], KV_LORA),
        'w_uq': nrm(ks[6], (L, Q_LORA, MLA_HEADS * QK_HEAD), Q_LORA),
        'w_ukv': nrm(ks[7], (L, KV_LORA, MLA_HEADS * (QK_NOPE + V_HEAD)), KV_LORA),
        'q_norm_g': gain(ks[8], QK_HEAD),
        'k_norm_g': gain(ks[9], QK_HEAD),
        'conv_w': nrm(ks[10], (L, CONV_K, CONV_WIDTH), CONV_K),
        'w_o_mla': nrm(ks[11], (L, MLA_HEADS * V_HEAD, D_MODEL), MLA_HEADS * V_HEAD),
        'w_o_conv': nrm(ks[12], (L, CONV_WIDTH, D_MODEL), CONV_WIDTH),
        'w_o': nrm(ks[13], (L, D_MODEL, D_MODEL), D_MODEL),
        'norm2_g': gain(ks[14], D_MODEL),
        'router_w': nrm(ks[15], (L, D_MODEL, N_EXPERTS), D_MODEL),
        'router_b': 0.01 * jax.random.normal(ks[16], (L, N_EXPERTS), jnp.float32),
        'expert_w1': nrm(ks[17], (L, N_EXPERTS, D_MODEL, 2 * D_FF), D_MODEL),
        'expert_b1': 0.01 * jax.random.normal(ks[18], (L, N_EXPERTS, 2 * D_FF), jnp.float32),
        'expert_w2': nrm(ks[19], (L, N_EXPERTS, D_FF, D_MODEL), D_FF),
        'expert_b2': 0.01 * jax.random.normal(ks[20], (L, N_EXPERTS, D_MODEL), jnp.float32),
    }

def reference(x, positions, norm1_g, w_in, q_a_norm_g, kv_a_norm_g, w_uq, w_ukv, q_norm_g, k_norm_g,
              conv_w, w_o_mla, w_o_conv, w_o, norm2_g, router_w, router_b,
              expert_w1, expert_b1, expert_w2, expert_b2):
    cos, sin = rope_tables(positions, x.dtype)
    for l in range(DEPTH):
        h = rms_norm(x, norm1_g[l])
        proj = h @ w_in[l]
        c_q, c_kv, k_rope, u, c_gate, b_gate, g_a, g_b = jnp.split(proj, IN_SPLITS, axis=-1)
        y_a = mla_branch(c_q, c_kv, k_rope, cos, sin, q_a_norm_g[l], kv_a_norm_g[l], w_uq[l], w_ukv[l],
                         q_norm_g[l], k_norm_g[l], w_o_mla[l])
        y_b = short_conv_branch(u, c_gate, b_gate, conv_w[l], w_o_conv[l])
        merged = jax.nn.sigmoid(g_a) * y_a + jax.nn.sigmoid(g_b) * y_b
        x = x + merged @ w_o[l]
        h2 = rms_norm(x, norm2_g[l])
        x = x + moe(h2, router_w[l], router_b[l], expert_w1[l], expert_b1[l], expert_w2[l], expert_b2[l])
    return x


_drawn_inputs = setup_inputs


def setup_inputs(seed=0):
    import zlib

    import numpy as np

    out = dict(_drawn_inputs(seed))
    spreads = {}
    factors = {'q_a_norm_g': 8.0,
     'kv_a_norm_g': 6.406,
     'q_norm_g': 8.0,
     'k_norm_g': 8.0,
     'expert_b1': 33.071,
     'expert_b2': 37.858,
     'norm2_g': 3.894,
     'router_b': 5.761}
    for name, (base, spread) in spreads.items():
        noise = np.random.default_rng([zlib.crc32(name.encode()), seed]).standard_normal(out[name].shape)
        drawn = base * np.exp(spread * noise) if base else spread * noise
        out[name] = __import__('jax').numpy.asarray(drawn.astype(out[name].dtype))
    for name, factor in factors.items():
        out[name] = (out[name] * factor).astype(out[name].dtype)
    return out
```

```python
import concourse.bass as bass
from concourse import mybir
from contextlib import ExitStack
import numpy as np

D, SEQ, P = 1024, 256, 128
TT, KT = SEQ // P, D // P
HEADS, NOPE, ROPE, VH = 8, 64, 32, 64
QK = NOPE + ROPE
HR = ROPE // 2
QL, KVL, CW = 256, 128, 512
A_COLS = QL + KVL + ROPE
CT = CW // P
EXPERTS, TOPK, FF = 32, 4, 1024
CH = 64
PASSES = SEQ // CH
KVX = NOPE + ROPE + VH
EPS = 1e-6
THETA = 10000.0
LIMIT, ALPHA = 7.0, 1.702


def build(nc, x, positions, norm1_g, w_in, q_a_norm_g, kv_a_norm_g, w_uq, w_ukv, q_norm_g, k_norm_g,
          conv_w, w_o_mla, w_o_conv, w_o, norm2_g, router_w, router_b, expert_w1, expert_b1,
          expert_w2, expert_b2, out):
    fp32, i32, u32 = mybir.dt.float32, mybir.dt.int32, mybir.dt.uint32
    ALU, ACT, AX = mybir.AluOpType, mybir.ActivationFunctionType, mybir.AxisListType
    ds = bass.ds

    ctx = ExitStack()
    with ctx:
        def sb(name, cols, dt=fp32, rows=P):
            return ctx.enter_context(nc.sbuf_tensor(name, [rows, cols], dt))

        def sem(name):
            return ctx.enter_context(nc.semaphore(name))

        def view(region, at, *shape, rows=P):
            n = int(np.prod(shape))
            part = region[0:rows, at:at + n]
            if len(shape) == 1:
                return part
            names = "abc"[:len(shape)]
            text = f"p ({' '.join(names)}) -> p {' '.join(names)}"
            return part.rearrange(text, **{c: s for c, s in zip(names[1:], shape[1:])})

        W1 = sb("W1", KT * 2 * FF)
        W2 = sb("W2", KT * D)
        WA = sb("WA", 9984)
        X = sb("X", TT * D)
        H = sb("H", TT * D)
        HT = sb("HT", KT * SEQ)
        ATT = sb("ATT", 9024)
        OT = sb("OT", 1024)
        YB = sb("YB", 1024)

        w1_sb = view(W1, 0, KT, 2 * FF)
        w2_sb = view(W2, 0, KT, D)
        w_gates = w1_sb
        w_uc = w2_sb
        w_mla = view(W2, 0, CT, D)
        w_cnv = view(W2, CT * D, CT, D)
        w_a = view(WA, 0, KT, A_COLS)
        w_uq_sb = view(WA, 3328, 2, HEADS * QK)
        w_ukv_sb = WA[:, 4864:5888]
        w_b = view(WA, 5888, KT, CW)
        w_o_sb = view(WA, 0, KT, D)
        cu = [view(WA, i * 258, 258) for i in range(2)]
        c_sb = [view(WA, 520 + i * 256, 256) for i in range(2)]
        y_tmp = [view(WA, 1032 + i * 256, 256) for i in range(2)]
        rot_tmp = [view(WA, 1600 + i * 256, TT, HEADS, HR) for i in range(4)]
        krot_tmp = [view(WA, 2640 + i * 32, TT, HR) for i in range(4)]

        x_sb = view(X, 0, TT, D)
        h_sb = view(H, 0, TT, D)
        sq_a = [H[:, 512 * t:512 * t + A_COLS] for t in range(TT)]
        sq_q = [view(H, 768 * t, HEADS, QK) for t in range(TT)]
        sq_k = [view(YB, 512 * t, HEADS, NOPE) for t in range(TT)]
        prob = [view(H, 512 * i, TT, SEQ) for i in range(2)]
        prob_t = [view(H, 1024 + 512 * i, TT, SEQ) for i in range(2)]
        sig = [view(H, 512 * i, 2, SEQ) for i in range(2)]
        gated = [view(H, 1024 + 512 * i, 2, SEQ) for i in range(2)]
        hT = view(HT, 0, KT, SEQ)

        q_sb = view(ATT, 0, TT, HEADS, QK)
        kvx = view(ATT, 1536, TT, HEADS, KVX)
        qT = view(ATT, 4096, HEADS, SEQ)
        kT = view(ATT, 6144, HEADS, SEQ)
        lat = view(ATT, 8192, TT, QL + KVL)
        krg = view(ATT, 8960, TT, ROPE)
        latT = view(OT, 0, 3, SEQ)
        oT = view(OT, 0, CT, SEQ)
        yT = view(YB, 0, CT, SEQ)
        rope_t = [view(YB, 32 * i, TT, HR) for i in range(8)]
        sq_x = YB[:, 0:D]

        mergedT = view(ATT, 0, KT, SEQ)
        xT = view(ATT, 2048, KT, CH)
        gate_sb, up_sb, sg_sb, y_sb = (ATT[:, 2560 + 512 * i:3072 + 512 * i] for i in range(4))
        actT = view(ATT, 4608, 4, P)
        pick = view(ATT, 5120, TT, CH)
        pick_w = view(ATT, 5248, TT, P)
        comb = view(ATT, 5504, TT, P)
        sel = ATT[0:2 * EXPERTS, 5760:5888]
        b1_sb = view(ATT, 5888, 2, 512, rows=2 * EXPERTS)
        b2_sb = ATT[0:EXPERTS, 6912:7936]
        half_mask = ATT[0:2 * EXPERTS, 7936:8064]
        rw_sb = view(ATT, 8064, KT, EXPERTS)
        logit = view(ATT, 8320, TT, EXPERTS)
        mask = view(ATT, 8384, TT, EXPERTS)
        ew = view(ATT, 8448, TT, EXPERTS)
        wd = view(ATT, 8512, TT, EXPERTS)
        rank = view(ATT, 8576, TT, EXPERTS + 1)
        wdT = ATT[0:EXPERTS, 8642:8898]
        one_hot = ATT[0:2 * EXPERTS, 8898:8898 + EXPERTS + 1]

        ident = sb("ident", P)
        before = sb("before", P)
        ones = sb("ones", P)
        slots = sb("slots", P)
        qg_sb, kg_sb = sb("qg_sb", QK), sb("kg_sb", QK)
        rb_sb = sb("rb_sb", EXPERTS)
        par = ATT[0:32, 0:P]
        pos_i = ATT[0:TT, P:2 * P].bitcast(i32)
        pos_f = ATT[0:TT, 2 * P:3 * P]
        parT = sb("parT", 34)
        invf = sb("invf", HR)
        mhalf = sb("mhalf", 32)
        cos_sb, sin_sb = sb("cos_sb", TT * HR), sb("sin_sb", TT * HR)
        ss, ms, rs = sb("ss", 48), sb("ms", 48), sb("rs", 48)
        rq = sb("rq", 16)
        mx, nm, sums, rsum = (sb(n, 16) for n in ("mx", "nm", "sums", "rsum"))
        top = sb("top", 16)
        topi = sb("topi", 16, u32)
        topf = sb("topf", 16)
        ntop, esum, ersum = sb("ntop", 2), sb("esum", 2), sb("ersum", 2)
        cmax = sb("cmax", 1)
        cmax_i = sb("cmax_i", 1, i32)
        krot = sb("krot", TT * ROPE)

        G1, G2, GL, GC = 0, 8, 16, 19

        bank = [ctx.enter_context(nc.psum_tensor(f"bank{i}", [P, 512], fp32)) for i in range(8)]
        GATE, UP, XTP, CTP, ATP, YP, COMB0, COMB1 = bank

        x_in = [sem(f"x_in{t}") for t in range(TT)]
        par_in, pos_in, gains_in, rb_in = sem("par_in"), sem("pos_in"), sem("gains_in"), sem("rb_in")
        wa_in = [sem(f"wa_in{i}") for i in range(2)]
        uq_in, ukv_in, b_in = sem("uq_in"), sem("ukv_in"), sem("b_in")
        uc_in = [sem(f"uc_in{i}") for i in range(2)]
        gates_in = [sem(f"gates_in{i}") for i in range(4)]
        mla_in, cnv_in = sem("mla_in"), sem("cnv_in")
        wo_in = [sem(f"wo_in{i}") for i in range(2)]
        router_in, b1_in, b2_in = sem("router_in"), sem("b1_in"), sem("b2_in")
        w1_in = [sem(f"w1_in{k}") for k in range(KT)]
        w2_in = [sem(f"w2_in{k}") for k in range(KT)]
        stored = [sem(f"stored{t}") for t in range(TT)]
        consts, consts2 = sem("consts"), sem("consts2")
        pool_step, dve_step = sem("pool_step"), sem("dve_step")
        pos_ready, par_tr, x_sq, ms_ready, rs_ready = (sem(n) for n in ("pos_ready", "par_tr", "x_sq", "ms_ready", "rs_ready"))
        h_ready, h_tr, hT_ready = sem("h_ready"), sem("h_tr"), sem("hT_ready")
        lat_mm, lat_sq, lat_ready, lat_tr, latT_ready = (sem(n) for n in ("lat_mm", "lat_sq", "lat_ready", "lat_tr", "latT_ready"))
        q_mm, kv_mm, q_sq, k_sq, q_out, k_out, v_out = (sem(n) for n in ("q_mm", "kv_mm", "q_sq", "k_sq", "q_out", "k_out", "v_out"))
        rope_ready = sem("rope_ready")
        q_ready, k_ready, q_tr, k_tr, qT_ready, kT_ready = (sem(n) for n in ("q_ready", "k_ready", "q_tr", "k_tr", "qT_ready", "kT_ready"))
        uc_mm, b_mm, c_out, yT_ready = sem("uc_mm"), sem("b_mm"), sem("c_out"), sem("yT_ready")
        s_mm, max_ready, exp_ready, p_norm, p_tr, pT_ready, o_mm, oT_ready = (
            sem(n) for n in ("s_mm", "max_ready", "exp_ready", "p_norm", "p_tr", "pT_ready", "o_mm", "oT_ready"))
        gate_mm, y_mm, sig_ready, merged = sem("gate_mm"), sem("y_mm"), sem("sig_ready"), sem("merged")
        x1_mm, x1_ready, x1_sq, h2_ready, h2_tr, h2T_ready = (
            sem(n) for n in ("x1_mm", "x1_ready", "x1_sq", "h2_ready", "h2_tr", "h2T_ready"))
        logit_mm, ntop_ready, ew_ready, mask_ready, rank_mm, count_ready = (
            sem(n) for n in ("logit_mm", "ntop_ready", "ew_ready", "mask_ready", "rank_mm", "count_ready"))
        wd_ready, wd_tr, wdT_ready, b2_mm = sem("wd_ready"), sem("wd_tr"), sem("wdT_ready"), sem("b2_mm")
        pick_ready, sel_ready, pickw_ready = sem("pick_ready"), sem("sel_ready"), sem("pickw_ready")
        gathered, xT_ready, bias_used, w1_used, w2_used = (sem(n) for n in ("gathered", "xT_ready", "bias_used", "w1_used", "w2_used"))
        gate_ready, up_ready, esig_ready, prod_ready, act_ready = (
            sem(n) for n in ("gate_ready", "up_ready", "esig_ready", "prod_ready", "act_ready"))
        pass_stored, rank_moved, pickw_tr, comb_ready, act_tr, actT_ready, y_ready, comb_mm, added = (
            sem(n) for n in ("pass_stored", "rank_moved", "pickw_tr", "comb_ready", "act_tr", "actT_ready", "y_ready", "comb_mm", "added"))

        block = ctx.enter_context(nc.Block())

        def rows(w):
            return w.rearrange("(k p) n -> p k n", p=P)

        @block.sync
        def _(sp):
            for t in range(TT):
                sp.dma_start(x_sb[:, t, :], x[0, t * P:(t + 1) * P, :]).then_inc(x_in[t], 16)
            wi = rows(w_in[0])
            for i in range(2):
                sp.dma_start(w_a[:, 4 * i:4 * i + 4, :], wi[:, 4 * i:4 * i + 4, 0:A_COLS]).then_inc(wa_in[i], 16)
            sp.dma_start(w_uq_sb, rows(w_uq[0])).then_inc(uq_in, 16)
            sp.dma_start(w_ukv_sb, w_ukv[0]).then_inc(ukv_in, 16)
            for i in range(2):
                sp.dma_start(w_uc[:, 4 * i:4 * i + 4, :],
                             wi[:, 4 * i:4 * i + 4, A_COLS:A_COLS + 2 * CW]).then_inc(uc_in[i], 16)
            sp.dma_start(w_b, wi[:, :, A_COLS + 2 * CW:A_COLS + 3 * CW]).then_inc(b_in, 16)
            for i in range(4):
                sp.dma_start(w_gates[:, 2 * i:2 * i + 2, :],
                             wi[:, 2 * i:2 * i + 2, A_COLS + 3 * CW:]).then_inc(gates_in[i], 16)
            sp.wait_ge(b_mm, CT)
            sp.dma_start(w_mla, rows(w_o_mla[0])).then_inc(mla_in, 16)
            sp.dma_start(w_cnv, rows(w_o_conv[0])).then_inc(cnv_in, 16)
            sp.wait_ge(yT_ready, CT)
            for i in range(2):
                sp.dma_start(w_o_sb[:, 4 * i:4 * i + 4, :], rows(w_o[0])[:, 4 * i:4 * i + 4, :]).then_inc(wo_in[i], 16)
            sp.wait_ge(o_mm, HEADS)
            sp.dma_start(rw_sb, rows(router_w[0])).then_inc(router_in, 16)
            for i in range(2):
                sp.dma_start(b1_sb[i * EXPERTS:(i + 1) * EXPERTS, :, :],
                             expert_b1[0].rearrange("e (s h n) -> e s h n", s=2, h=2)[:, :, i, :]).then_inc(b1_in, 16)
            sp.dma_start(b2_sb, expert_b2[0]).then_inc(b2_in, 16)

            def load_experts(c):
                with sp.Fori(0, EXPERTS) as e:
                    n = e + EXPERTS * c
                    for k in range(KT):
                        sp.wait_ge(w1_used, n * KT + (k + 1))
                        sp.dma_start(w1_sb[:, k, :], expert_w1[0, ds(e, 1), k * P:(k + 1) * P, :].rearrange("a p n -> p (a n)")).then_inc(w1_in[k], 16)
                    for k in range(KT):
                        sp.wait_ge(w2_used, n * KT + (k + 1))
                        sp.dma_start(w2_sb[:, k, :], expert_w2[0, ds(e, 1), k * P:(k + 1) * P, :].rearrange("a p n -> p (a n)")).then_inc(w2_in[k], 16)

            load_experts(0)
            sp.wait_ge(count_ready, 1)
            most = sp.value_load(cmax_i[0:1, 0:1], min_val=0, max_val=SEQ)
            with sp.If(most > CH):
                with sp.Fori(1, PASSES) as c:
                    with sp.If(most > c * CH):
                        load_experts(c)
                        sp.wait_ge(added, c * (2 * EXPERTS) + (2 * EXPERTS + 2))
                        sp.sem_inc(pass_stored, 1)
            for t in range(TT):
                sp.wait_ge(added, 2 * EXPERTS + 1 + t)
                sp.dma_start(out[0, t * P:(t + 1) * P, :], x_sb[:, t, :]).then_inc(stored[t], 16)
            for t in range(TT):
                sp.wait_ge(stored[t], 16)

        @block.gpsimd
        def _(pool):
            n = [0]

            def link(ins):
                n[0] += 1
                ins.then_inc(pool_step, 1)
                pool.wait_ge(pool_step, n[0])

            pool.memset(ident[:, :], 0.0)
            link(pool.memset(before[:, :], 1.0))
            pool.affine_select(out=ident[:, :], in_=ident[:, :], compare_op=ALU.not_equal, fill=1.0,
                               base=0, pattern=[[-1, P]], channel_multiplier=1).then_inc(consts, 1)
            pool.memset(mhalf[:, :], -0.5)
            inv = np.float32(THETA) ** (-np.arange(0, ROPE, 2, dtype=np.float32) / np.float32(ROPE))
            for i in range(HR):
                last = pool.memset(invf[:, i:i + 1], float(inv[i]))
            link(last)
            pool.affine_select(out=before[:, :], in_=before[:, :], compare_op=ALU.is_gt, fill=0.0,
                               base=0, pattern=[[1, P]], channel_multiplier=-1)
            pool.memset(ones[:, :], 1.0)
            pool.iota(slots[:, :], pattern=[[0, 2], [1, CH]], base=0, channel_multiplier=0,
                      allow_small_or_imprecise_dtypes=True).then_inc(consts, 1)

            def power(at, width, k):
                pool.wait_ge(ms_ready, k)
                pool.tensor_tensor(rs[:, at:at + width], ms[:, at:at + width], mhalf[:, 0:width],
                                   ALU.pow).then_inc(rs_ready, 1)

            for t in range(TT):
                power(t, 1, 1 + t)
            for t in range(TT):
                power(2 + 2 * t, 2, 3 + t)
            power(8, 32, 5)
            pool.wait_ge(o_mm, HEADS)
            link(pool.memset(rank[:, :, EXPERTS:EXPERTS + 1], -1.0))
            for i in range(2):
                rows_i = slice(i * EXPERTS, (i + 1) * EXPERTS)
                link(pool.memset(half_mask[rows_i, i * CH:(i + 1) * CH], 1.0))
                link(pool.memset(half_mask[rows_i, (1 - i) * CH:(2 - i) * CH], 0.0))
            link(pool.memset(one_hot, 0.0))
            for i in range(2):
                part = one_hot[i * EXPERTS:(i + 1) * EXPERTS, :]
                link(pool.affine_select(out=part, in_=part, compare_op=ALU.not_equal, fill=1.0,
                                        base=0, pattern=[[-1, EXPERTS + 1]], channel_multiplier=1))
            pool.sem_inc(consts2, 1)
            for t in range(TT):
                power(40 + t, 1, 6 + t)

        @block.scalar
        def _(act):
            act.dma_start(pos_i[:, :], positions[0].rearrange("(t p) -> t p", p=P)).then_inc(pos_in, 16)
            act.dma_start(par[G1:G1 + 8, :], norm1_g[0].rearrange("(k p) -> k p", p=P)).then_inc(par_in, 16)
            act.dma_start(par[G2:G2 + 8, :], norm2_g[0].rearrange("(k p) -> k p", p=P)).then_inc(par_in, 16)
            act.dma_start(par[GL:GL + 2, :], q_a_norm_g[0].rearrange("(k p) -> k p", p=P)).then_inc(par_in, 16)
            act.dma_start(par[GL + 2:GL + 3, :], kv_a_norm_g[0].rearrange("(k p) -> k p", p=P)).then_inc(par_in, 16)
            act.dma_start(par[GC:GC + 12, :], conv_w[0].rearrange("w (k p) -> (w k) p", p=P)).then_inc(par_in, 16)
            act.dma_start(qg_sb[:, :], q_norm_g[0].partition_broadcast(P)).then_inc(gains_in, 16)
            act.dma_start(kg_sb[:, :], k_norm_g[0].partition_broadcast(P)).then_inc(gains_in, 16)
            act.dma_start(rb_sb[:, :], router_b[0].partition_broadcast(P)).then_inc(rb_in, 16)
            for t in range(TT):
                act.wait_ge(x_in[t], 16)
                act.activation(HT[:, t * D:(t + 1) * D], x_sb[:, t, :], ACT.Square,
                               accum_out=ss[:, t:t + 1]).then_inc(x_sq, 1)
            for t in range(TT):
                act.wait_ge(lat_mm, t + 1)
                for a, b, col in ((0, QL, 2 + 2 * t), (QL, QL + KVL, 3 + 2 * t), (QL + KVL, A_COLS, 6 + t)):
                    last = act.activation(sq_a[t][:, a:b], bank[4 + t][:, a:b], ACT.Square, accum_out=ss[:, col:col + 1])
                last.then_inc(lat_sq, 1)
            for t in range(TT):
                act.wait_ge(q_mm, t + 1)
                for i in range(2):
                    last = act.activation(sq_q[t][:, 4 * i:4 * i + 4, :],
                                          bank[2 * t + i][:, 0:4 * QK].rearrange("p (h d) -> p h d", d=QK), ACT.Square)
                last.then_inc(q_sq, 1)
            for t in range(TT):
                act.wait_ge(kv_mm, t + 1)
                for i in range(2):
                    kv = bank[4 + 2 * t + i][:, :].rearrange("p (h d) -> p h d", d=NOPE + VH)
                    last = act.activation(sq_k[t][:, 4 * i:4 * i + 4, :], kv[:, :, 0:NOPE], ACT.Square)
                last.then_inc(k_sq, 1)
                for i in range(2):
                    kv = bank[4 + 2 * t + i][:, :].rearrange("p (h d) -> p h d", d=NOPE + VH)
                    last = act.activation(kvx[:, t, 4 * i:4 * i + 4, QK:KVX], kv[:, :, NOPE:], ACT.Copy)
                last.then_inc(v_out, 1)

            def conv_c(f):
                act.wait_ge(uc_mm, f + 1)
                if f >= 2:
                    act.wait_ge(yT_ready, f - 1)
                act.activation(c_sb[f % 2], bank[2 * (f % 2)][:, SEQ:2 * SEQ], ACT.Copy).then_inc(c_out, 1)

            conv_c(0)
            for i in range(4):
                t, g = i // 2, i % 2
                act.wait_ge(q_tr, i + 1)
                act.activation(qT[0:QK, 4 * g:4 * g + 4, t * P:(t + 1) * P],
                               bank[4 + i][0:QK, :].rearrange("p (h s) -> p h s", s=P), ACT.Copy).then_inc(qT_ready, 1)

            def head_exp(h):
                act.wait_ge(max_ready, h + 1)
                if h >= 2:
                    act.wait_ge(p_tr, h - 1)
                for t in range(TT):
                    c = TT * h + t
                    last = act.activation(prob[h % 2][:, t, :], bank[4 + h % 2][:, t * SEQ:(t + 1) * SEQ], ACT.Exp,
                                          bias=nm[:, c:c + 1], scale=rq[:, c:c + 1], accum_out=sums[:, c:c + 1])
                last.then_inc(exp_ready, 1)

            head_exp(0)
            conv_c(1)
            for h in range(HEADS):
                if h + 1 < HEADS:
                    head_exp(h + 1)
                act.wait_ge(p_tr, h + 1)
                act.activation(prob_t[h % 2], bank[6][:, :].rearrange("p (k s) -> p k s", s=SEQ), ACT.Copy).then_inc(pT_ready, 1)
                if h % 2:
                    act.wait_ge(o_mm, h + 1)
                    act.activation(oT[:, h // 2, :], bank[7][:, 0:SEQ], ACT.Copy).then_inc(oT_ready, 1)
                if h in (3, 6):
                    conv_c(2 if h == 3 else 3)
            for d in range(KT):
                act.wait_ge(gate_mm, d + 1)
                if d >= 2:
                    act.wait_ge(merged, d - 1)
                act.activation(sig[d % 2], bank[2 * (d % 2)][:, :].rearrange("p (g s) -> p g s", s=SEQ), ACT.Sigmoid).then_inc(sig_ready, 1)
            for t in range(TT):
                act.wait_ge(x1_ready, t + 1)
                act.activation(sq_x, x_sb[:, t, :], ACT.Square, accum_out=ss[:, 40 + t:41 + t]).then_inc(x1_sq, 1)
            for t in range(TT):
                act.wait_ge(ntop_ready, t + 1)
                act.activation(ew[:, t, :], logit[:, t, :], ACT.Exp, bias=ntop[:, t:t + 1]).then_inc(ew_ready, 1)
            act.wait_ge(wd_tr, 1)
            act.activation(wdT, bank[7][0:EXPERTS, 0:SEQ], ACT.Copy).then_inc(wdT_ready, 1)

            def experts(c):
                with act.Fori(0, EXPERTS) as e:
                    n = e + EXPERTS * c
                    act.wait_ge(gate_ready, n + 1)
                    act.activation(sg_sb, gate_sb, ACT.Sigmoid, scale=ALPHA).then_inc(esig_ready, 1)
                    act.wait_ge(pickw_tr, n + 1)
                    act.activation(comb, CTP[:, 0:SEQ].rearrange("p (t s) -> p t s", s=P), ACT.Copy).then_inc(comb_ready, 1)
                    act.wait_ge(act_tr, n + 1)
                    act.activation(actT, ATP[:, :].rearrange("p (j s) -> p j s", s=P), ACT.Copy).then_inc(actT_ready, 1)

            experts(0)
            act.wait_ge(count_ready, 1)
            most = act.value_load(cmax_i[0:1, 0:1], min_val=0, max_val=SEQ)
            with act.If(most > CH):
                with act.Fori(1, PASSES) as c:
                    with act.If(most > c * CH):
                        experts(c)

        @block.tensor
        def _(pe):
            pe.wait_ge(consts, 1)
            pe.wait_ge(par_in, 80)
            pe.wait_ge(pos_ready, 1)
            pe.transpose(bank[7][:, 0:31], par[0:31, :], ident[0:31, 0:31])
            pe.transpose(bank[7][:, 32:34], pos_f[:, :], ident[0:TT, 0:TT]).then_inc(par_tr, 1)
            for t in range(TT):
                pe.wait_ge(h_ready, t + 1)
                for k in range(KT):
                    last = pe.transpose(bank[2 * t + k // 4][:, (k % 4) * P:(k % 4 + 1) * P], h_sb[:, t, k * P:(k + 1) * P], ident[:, :])
                    if k % 4 == 3:
                        last.then_inc(h_tr, 1)
            for t in range(TT):
                pe.wait_ge(hT_ready, 2 * t + 2)
                for k in range(KT):
                    pe.wait_ge(wa_in[k // 4], 16)
                    last = pe.matmul(bank[4 + t][:, 0:A_COLS], hT[:, k, t * P:(t + 1) * P], w_a[:, k, :], start=(k == 0), stop=(k == KT - 1))
                last.then_inc(lat_mm, 1)
            for t in range(TT):
                pe.wait_ge(lat_ready, t + 1)
                for k in range(3):
                    last = pe.transpose(bank[6 + t][:, k * P:(k + 1) * P], lat[:, t, k * P:(k + 1) * P], ident[:, :])
                last.then_inc(lat_tr, 1)
            pe.wait_ge(uq_in, 16)
            for t in range(TT):
                pe.wait_ge(latT_ready, t + 1)
                for i in range(2):
                    for k in range(2):
                        last = pe.matmul(bank[2 * t + i][:, 0:4 * QK], latT[:, k, t * P:(t + 1) * P],
                                         w_uq_sb[:, k, i * 4 * QK:(i + 1) * 4 * QK], start=(k == 0), stop=(k == 1))
                last.then_inc(q_mm, 1)
            pe.wait_ge(ukv_in, 16)
            for t in range(TT):
                for i in range(2):
                    last = pe.matmul(bank[4 + 2 * t + i][:, :], latT[:, 2, t * P:(t + 1) * P], w_ukv_sb[:, 512 * i:512 * i + 512], start=True, stop=True)
                last.then_inc(kv_mm, 1)

            def conv_group(i):
                f, part = divmod(i, 3)
                pair = 2 * (f % 2)
                if part == 0:
                    if f < 2:
                        pe.wait_ge(q_out, f + 1)
                        pe.wait_ge(q_sq, f + 1)
                    else:
                        pe.wait_ge(yT_ready, f - 1)
                dst = bank[pair + part // 2][:, (part % 2) * SEQ:(part % 2 + 1) * SEQ]
                for k in range(KT):
                    if part == 2:
                        pe.wait_ge(b_in, 16)
                        w = w_b[:, k, f * P:(f + 1) * P]
                    else:
                        pe.wait_ge(uc_in[k // 4], 16)
                        w = w_uc[:, k, part * CW + f * P:part * CW + (f + 1) * P]
                    last = pe.matmul(dst, w, hT[:, k, :], start=(k == 0), stop=(k == KT - 1))
                if part == 1:
                    last.then_inc(uc_mm, 1)
                elif part == 2:
                    last.then_inc(b_mm, 1)

            def head_scores(h):
                if h >= 2:
                    pe.wait_ge(exp_ready, h - 1)
                for t in range(TT):
                    last = pe.matmul(bank[4 + h % 2][:, t * SEQ:(t + 1) * SEQ], qT[0:QK, h, t * P:(t + 1) * P], kT[0:QK, h, :], start=True, stop=True)
                last.then_inc(s_mm, 1)

            for i in range(4):
                conv_group(i)
            pe.wait_ge(q_ready, 1)
            pe.wait_ge(k_out, 2)
            pe.wait_ge(v_out, 2)
            for i in range(4):
                t, g = i // 2, i % 2
                for h in range(4):
                    last = pe.transpose(bank[4 + i][0:QK, h * P:(h + 1) * P], q_sb[:, t, 4 * g + h, :], ident[:, :])
                last.then_inc(q_tr, 1)
            conv_group(4)
            pe.wait_ge(k_ready, 1)
            for i in range(4):
                t, g = i // 2, i % 2
                pe.wait_ge(qT_ready, i + 1)
                for h in range(4):
                    last = pe.transpose(bank[4 + i][0:QK, h * P:(h + 1) * P], kvx[:, t, 4 * g + h, 0:QK], ident[:, :])
                last.then_inc(k_tr, 1)
            pe.wait_ge(kT_ready, 4)
            head_scores(0)
            for h in range(HEADS):
                if h + 1 < HEADS:
                    head_scores(h + 1)
                if 5 + h < 3 * CT:
                    conv_group(5 + h)
                pe.wait_ge(p_norm, h + 1)
                if h >= 1:
                    pe.wait_ge(pT_ready, h)
                for t in range(TT):
                    for k in range(TT):
                        last = pe.transpose(bank[6][:, k * SEQ + t * P:k * SEQ + (t + 1) * P], prob[h % 2][:, t, k * P:(k + 1) * P], ident[:, :])
                last.then_inc(p_tr, 1)
                pe.wait_ge(pT_ready, h + 1)
                if h >= 2 and h % 2 == 0:
                    pe.wait_ge(oT_ready, h // 2)
                for k in range(TT):
                    last = pe.matmul(bank[7][VH * (h % 2):VH * (h % 2) + VH, 0:SEQ], kvx[:, k, h, QK:KVX], prob_t[h % 2][:, k, :], start=(k == 0), stop=(k == TT - 1))
                last.then_inc(o_mm, 1)

            for d in range(KT):
                cols = slice(d * P, (d + 1) * P)
                gb, yb = bank[2 * (d % 2)], bank[2 * (d % 2) + 1]
                if d < 2:
                    pe.wait_ge(yT_ready, d + 3)
                else:
                    pe.wait_ge(merged, d - 1)
                for g in range(2):
                    for k in range(KT):
                        pe.wait_ge(gates_in[k // 2], 16)
                        last = pe.matmul(gb[:, g * SEQ:(g + 1) * SEQ], w_gates[:, k, g * D + d * P:g * D + (d + 1) * P], hT[:, k, :], start=(k == 0), stop=(k == KT - 1))
                last.then_inc(gate_mm, 1)
                pe.wait_ge(oT_ready, CT)
                pe.wait_ge(yT_ready, CT)
                pe.wait_ge(mla_in, 16)
                pe.wait_ge(cnv_in, 16)
                for g, (w, v) in enumerate(((w_mla, oT), (w_cnv, yT))):
                    for k in range(CT):
                        last = pe.matmul(yb[:, g * SEQ:(g + 1) * SEQ], w[:, k, cols], v[:, k, :], start=(k == 0), stop=(k == CT - 1))
                        if d == KT - 1 and g == 0 and k == 0:
                            last.then_inc(w1_used, KT)
                last.then_inc(y_mm, 1)
            for t in range(TT):
                for i in range(2):
                    for k in range(KT):
                        if t == 0 and i == 0:
                            pe.wait_ge(merged, k + 1)
                            pe.wait_ge(wo_in[k // 4], 16)
                        last = pe.matmul(bank[4 + 2 * t + i][:, :], mergedT[:, k, t * P:(t + 1) * P], w_o_sb[:, k, 512 * i:512 * i + 512], start=(k == 0), stop=(k == KT - 1))
                        if t == 0 and i == 0 and k == 0:
                            last.then_inc(w2_used, KT)
                    last.then_inc(x1_mm, 1)
            for t in range(TT):
                pe.wait_ge(h2_ready, t + 1)
                for k in range(KT):
                    last = pe.transpose(bank[2 * t + k // 4][:, (k % 4) * P:(k % 4 + 1) * P], h_sb[:, t, k * P:(k + 1) * P], ident[:, :])
                    if k % 4 == 3:
                        last.then_inc(h2_tr, 1)
            pe.wait_ge(router_in, 16)
            for t in range(TT):
                pe.wait_ge(h2T_ready, 2 * t + 2)
                for k in range(KT):
                    last = pe.matmul(bank[4 + 2 * t][:, 0:EXPERTS], hT[:, k, t * P:(t + 1) * P], rw_sb[:, k, :], start=(k == 0), stop=(k == KT - 1))
                last.then_inc(logit_mm, 1)
            pe.wait_ge(mask_ready, 2)
            pe.matmul(bank[5][:, 0:EXPERTS], before[:, :], mask[:, 0, :], start=True, stop=True)
            pe.matmul(bank[5][:, EXPERTS:2 * EXPERTS], ones[:, :], mask[:, 0, :], start=True, stop=False)
            pe.matmul(bank[5][:, EXPERTS:2 * EXPERTS], before[:, :], mask[:, 1, :], start=False, stop=True)
            pe.matmul(bank[5][:, 2 * EXPERTS:3 * EXPERTS], ones[:, :], mask[:, 0, :], start=True, stop=False)
            pe.matmul(bank[5][:, 2 * EXPERTS:3 * EXPERTS], ones[:, :], mask[:, 1, :], start=False, stop=True).then_inc(rank_mm, 1)

            def gather(count):
                pe.wait_ge(pick_ready, count)
                for k in range(KT):
                    for t in range(TT):
                        last = pe.matmul(XTP[:, k * CH:(k + 1) * CH], h_sb[:, t, k * P:(k + 1) * P], pick[:, t, :], start=(t == 0), stop=(t == TT - 1))
                last.then_inc(gathered, 1)

            def experts(c):
                first = c * (EXPERTS + 1)
                if isinstance(c, int):
                    gather(1)
                    pe.wait_ge(wd_ready, 1)
                    for t in range(TT):
                        last = pe.transpose(bank[7][0:EXPERTS, t * P:(t + 1) * P], wd[:, t, :], ident[:, :])
                    last.then_inc(wd_tr, 1)
                    pe.wait_ge(wdT_ready, 1)
                    pe.wait_ge(b2_in, 16)
                    for t, i, dst in ((0, 0, COMB0), (0, 1, COMB1), (1, 0, CTP), (1, 1, ATP)):
                        last = pe.matmul(dst[:, :], wdT[:, t * P:(t + 1) * P], b2_sb[:, 512 * i:512 * i + 512], start=True, stop=True)
                        if i:
                            last.then_inc(b2_mm, 1)
                    pe.wait_ge(b1_in, 32)
                else:
                    pe.wait_ge(xT_ready, first)
                    gather(first + 1)
                with pe.Fori(0, EXPERTS) as e:
                    n = e + EXPERTS * c
                    pe.wait_ge(xT_ready, first + e + 1)
                    pe.wait_ge(sel_ready, first + e + 1)
                    pe.matmul(GATE[:, :], sel, b1_sb[:, 0, :], start=True, stop=True)
                    pe.matmul(UP[:, :], sel, b1_sb[:, 1, :], start=True, stop=True).then_inc(bias_used, 1)
                    for k in range(KT):
                        pe.wait_ge(w1_in[k], n * 16 + 16)
                        for s, dst in enumerate((GATE, UP)):
                            for g in range(2):
                                at = s * FF + g * 512
                                last = pe.matmul(dst[g * CH:(g + 1) * CH, :], xT[:, k, :], w1_sb[:, k, at:at + 512], start=False, stop=True, skip_group_check=True)
                        last.then_inc(w1_used, 1)
                    gather(first + e + 2)
                    pe.wait_ge(pickw_ready, n + 1)
                    pe.wait_ge(added, n * 2 + 2)
                    for t in range(TT):
                        last = pe.transpose(CTP[:, t * P:(t + 1) * P], pick_w[:, t, :], ident[:, :])
                    last.then_inc(pickw_tr, 1)
                    pe.wait_ge(act_ready, n + 1)
                    for j in range(4):
                        last = pe.transpose(ATP[:, j * P:(j + 1) * P], up_sb[:, j * P:(j + 1) * P], ident[:, :])
                    last.then_inc(act_tr, 1)
                    pe.wait_ge(actT_ready, n + 1)
                    for k in range(KT):
                        pe.wait_ge(w2_in[k], n * 16 + 16)
                        g, j = divmod(k, 4)
                        for i in range(2):
                            last = pe.matmul(YP[i * CH:(i + 1) * CH, :], actT[:, j, g * CH:(g + 1) * CH], w2_sb[:, k, 512 * i:512 * i + 512], start=(k == 0), stop=(k == KT - 1))
                        last.then_inc(w2_used, 1)
                    pe.wait_ge(y_ready, n + 1)
                    pe.wait_ge(comb_ready, n + 1)
                    for t, dsts in enumerate(((COMB0, COMB1), (CTP, ATP))):
                        for i in range(2):
                            half = slice(i * CH, (i + 1) * CH)
                            last = pe.matmul(dsts[i][:, :], comb[half, t, :], y_sb[half, :], start=True, stop=True)
                        last.then_inc(comb_mm, 1)

            experts(0)
            pe.wait_ge(count_ready, 1)
            most = pe.value_load(cmax_i[0:1, 0:1], min_val=0, max_val=SEQ)
            with pe.If(most > CH):
                with pe.Fori(1, PASSES) as c:
                    with pe.If(most > c * CH):
                        experts(c)

        @block.vector
        def _(dve):
            n_step = [0]

            def link(ins):
                n_step[0] += 1
                ins.then_inc(dve_step, 1)
                dve.wait_ge(dve_step, n_step[0])

            def bc(ap, *shape):
                return ap.to_broadcast(list(shape))

            mult, add, sub = ALU.mult, ALU.add, ALU.subtract
            dve.wait_ge(pos_in, 16)
            dve.tensor_copy(pos_f[:, :], pos_i[:, :]).then_inc(pos_ready, 1)

            def scaled(col, width, size, last=True):
                i = dve.tensor_scalar(ms[:, col:col + width], ss[:, col:col + width], 1.0 / size, EPS, mult, add)
                if last:
                    i.then_inc(ms_ready, 1)

            for t in range(TT):
                dve.wait_ge(x_sq, t + 1)
                scaled(t, 1, D)
            dve.wait_ge(par_tr, 1)
            dve.tensor_copy(parT[:, 0:31], bank[7][:, 0:31])
            link(dve.tensor_copy(parT[:, 32:34], bank[7][:, 32:34]))
            for t in range(TT):
                dve.wait_ge(rs_ready, t + 1)
                dve.tensor_scalar(h_sb[:, t, :], x_sb[:, t, :], rs[:, t:t + 1], None, mult).then_inc(h_ready, 1)

            def norm_out(t, i, g, done):
                dve.tensor_tensor(hT[:, 4 * i:4 * i + 4, t * P:(t + 1) * P], bank[2 * t + i][:, :].rearrange("p (k s) -> p k s", s=P),
                                  bc(parT[:, g + 4 * i:g + 4 * i + 4].unsqueeze(2), P, 4, P), mult).then_inc(done, 1)

            for t in range(TT):
                for i in range(2):
                    dve.wait_ge(h_tr, 2 * t + i + 1)
                    norm_out(t, i, G1, hT_ready)

            dve.wait_ge(consts, 2)
            ang, kk, r, z, sp_, cp_, sn_, cs_ = rope_t
            for t in range(TT):
                last = dve.tensor_scalar(ang[:, t, :], invf[:, :], parT[:, 32 + t:33 + t], None, mult)
            link(last)
            two_pi = 2 * np.pi
            c1 = 6.28125
            c2 = float(np.round((two_pi - c1) * 2 ** 17) / 2 ** 17)
            c3 = two_pi - c1 - c2
            magic = 1.5 * 2 ** 23
            link(dve.tensor_scalar(kk, ang, 1 / two_pi, magic, mult, add))
            link(dve.tensor_scalar(kk, kk, -magic, None, add))
            link(dve.scalar_tensor_tensor(r, kk, -c1, ang, mult, add))
            link(dve.scalar_tensor_tensor(r, kk, -c2, r, mult, add))
            link(dve.scalar_tensor_tensor(r, kk, -c3, r, mult, add))
            link(dve.tensor_scalar(r, r, 0.5, None, mult))
            link(dve.tensor_tensor(z, r, r, mult))
            s_c, c_c, f = [], [], 1.0
            for i in range(1, 14):
                f *= i
                (s_c if i % 2 else c_c).append((-1) ** (i // 2) / f)
            s_c = s_c[1:]
            dve.tensor_scalar(sp_, z, s_c[-1], None, mult)
            link(dve.tensor_scalar(cp_, z, c_c[-1], None, mult))
            for i in range(len(s_c) - 2, -1, -1):
                dve.scalar_tensor_tensor(sp_, sp_, s_c[i], z, add, mult)
                link(dve.scalar_tensor_tensor(cp_, cp_, c_c[i], z, add, mult))
            dve.scalar_tensor_tensor(sn_, sp_, 1.0, r, add, mult)
            link(dve.tensor_scalar(cs_, cp_, 1.0, None, add))
            cos_t, sin_t = (v[:, :].rearrange("p (t r) -> p t r", t=TT) for v in (cos_sb, sin_sb))
            dve.scalar_tensor_tensor(sin_t, sn_, 2.0, cs_, mult, mult)
            link(dve.scalar_tensor_tensor(cos_t, sn_, -2.0, sn_, mult, mult))
            link(dve.tensor_scalar(cos_t, cos_t, 1.0, None, add))

            dve.wait_ge(gains_in, 32)
            for t in range(TT):
                dve.wait_ge(lat_sq, t + 1)
                scaled(2 + 2 * t, 1, QL, last=False)
                scaled(3 + 2 * t, 1, KVL)
            for t in range(TT):
                dve.tensor_tensor(krg[:, t, :], bank[4 + t][:, QL + KVL:A_COLS], kg_sb[:, NOPE:QK], mult)
                dve.wait_ge(rs_ready, 3 + t)
                dve.tensor_scalar(lat[:, t, 0:QL], bank[4 + t][:, 0:QL], rs[:, 2 + 2 * t:3 + 2 * t], None, mult)
                dve.tensor_scalar(lat[:, t, QL:], bank[4 + t][:, QL:QL + KVL], rs[:, 3 + 2 * t:4 + 2 * t], None, mult).then_inc(lat_ready, 1)
            for t in range(TT):
                dve.wait_ge(lat_tr, t + 1)
                dve.tensor_tensor(latT[:, :, t * P:(t + 1) * P], bank[6 + t][:, 0:3 * P].rearrange("p (k s) -> p k s", s=P),
                                  bc(parT[:, GL:GL + 3].unsqueeze(2), P, 3, P), mult).then_inc(latT_ready, 1)

            def rotate(src, tmp, dst, cos, sin, shape):
                t1, t2 = src(0), src(1)
                dve.tensor_tensor(tmp[0], t1, cos, mult)
                dve.tensor_tensor(tmp[1], t2, sin, mult)
                dve.tensor_tensor(tmp[2], t1, sin, mult)
                link(dve.tensor_tensor(tmp[3], t2, cos, mult))
                dve.tensor_tensor(dst(0), tmp[0], tmp[1], sub)
                return dve.tensor_tensor(dst(1), tmp[2], tmp[3], add)

            link(rotate(lambda i: krg[:, :, i * HR:(i + 1) * HR], krot_tmp,
                        lambda i: krot[:, :].rearrange("p (t r) -> p t r", t=TT)[:, :, i * HR:(i + 1) * HR],
                        cos_t, sin_t, None))
            for t in range(TT):
                dve.wait_ge(q_sq, t + 1)
                for i in range(2):
                    last = dve.tensor_tensor(q_sb[:, t, 4 * i:4 * i + 4, :], bank[2 * t + i][:, 0:4 * QK].rearrange("p (h d) -> p h d", d=QK),
                                             bc(qg_sb[:, :].unsqueeze(1), P, 4, QK), mult)
                last.then_inc(q_out, 1)
            for t in range(TT):
                dve.tensor_reduce(ss[:, 8 + 8 * t:16 + 8 * t], sq_q[t], AX.X, add)
            for t in range(TT):
                dve.wait_ge(v_out, t + 1)
                for i in range(2):
                    kv = bank[4 + 2 * t + i][:, :].rearrange("p (h d) -> p h d", d=NOPE + VH)
                    last = dve.tensor_tensor(kvx[:, t, 4 * i:4 * i + 4, 0:NOPE], kv[:, :, 0:NOPE],
                                             bc(kg_sb[:, 0:NOPE].unsqueeze(1), P, 4, NOPE), mult)
                last.then_inc(k_out, 1)
            for t in range(TT):
                last = dve.tensor_reduce(ss[:, 24 + 8 * t:32 + 8 * t], sq_k[t], AX.X, add)
            link(last)
            for t in range(TT):
                last = dve.tensor_scalar(ss[:, 24 + 8 * t:32 + 8 * t], ss[:, 24 + 8 * t:32 + 8 * t], ss[:, 6 + t:7 + t], None, add)
            link(last)
            scaled(8, 32, QK)
            wide = [bc(v.unsqueeze(2), P, TT, HEADS, HR) for v in (cos_t, sin_t)]
            half = lambda i: q_sb[:, :, :, NOPE + i * HR:NOPE + (i + 1) * HR]
            dve.wait_ge(q_out, 2)
            rotate(half, rot_tmp, half, wide[0], wide[1], None).then_inc(q_ready, 1)
            dve.wait_ge(rs_ready, 5)
            dve.wait_ge(k_out, 2)
            for t in range(TT):
                rk = rs[:, 24 + 8 * t:32 + 8 * t].unsqueeze(2)
                dve.tensor_tensor(kvx[:, t, :, 0:NOPE], kvx[:, t, :, 0:NOPE], bc(rk, P, HEADS, NOPE), mult)
                last = dve.tensor_tensor(kvx[:, t, :, NOPE:QK], bc(krot[:, t * ROPE:(t + 1) * ROPE].unsqueeze(1), P, HEADS, ROPE),
                                         bc(rk, P, HEADS, ROPE), mult)
            last.then_inc(k_ready, 1)
            link(dve.tensor_scalar(rq[:, :].rearrange("p (h t) -> p t h", t=TT), rs[:, 8:24].rearrange("p (t h) -> p t h", t=TT),
                                   float(QK) ** -0.5, None, mult))

            def conv(f):
                u, b = bank[2 * (f % 2)][:, 0:SEQ], bank[2 * (f % 2) + 1][:, 0:SEQ]
                c, y = cu[f % 2], y_tmp[f % 2]
                w = [parT[:, GC + CT * i + f:GC + CT * i + f + 1] for i in range(3)]
                if f < 2:
                    dve.memset(c[:, 0:1], 0.0)
                    dve.memset(c[:, SEQ + 1:SEQ + 2], 0.0)
                dve.wait_ge(c_out, f + 1)
                link(dve.tensor_tensor(c[:, 1:SEQ + 1], u, c_sb[f % 2], mult))
                link(dve.tensor_scalar(y, c[:, 0:SEQ], w[0], None, mult))
                link(dve.scalar_tensor_tensor(y, c[:, 1:SEQ + 1], w[1], y, mult, add))
                link(dve.scalar_tensor_tensor(y, c[:, 2:SEQ + 2], w[2], y, mult, add))
                dve.wait_ge(b_mm, f + 1)
                dve.tensor_tensor(yT[:, f, :], b, y, mult).then_inc(yT_ready, 1)

            def head_max(h):
                dve.wait_ge(s_mm, h + 1)
                pair = slice(TT * h, TT * h + TT)
                link(dve.tensor_reduce(mx[:, pair], bank[4 + h % 2][:, :].rearrange("p (t s) -> p t s", t=TT), AX.X, ALU.max))
                dve.scalar_tensor_tensor(nm[:, pair], mx[:, pair], -1.0, rq[:, pair], mult, mult).then_inc(max_ready, 1)

            def head_norm(h):
                dve.wait_ge(exp_ready, h + 1)
                pair = slice(TT * h, TT * h + TT)
                link(dve.reciprocal(rsum[:, pair], sums[:, pair]))
                for t in range(TT):
                    last = dve.tensor_scalar(prob[h % 2][:, t, :], prob[h % 2][:, t, :], rsum[:, TT * h + t:TT * h + t + 1], None, mult)
                last.then_inc(p_norm, 1)

            conv(0)
            for i in range(4):
                t, g = i // 2, i % 2
                dve.wait_ge(k_tr, i + 1)
                dve.tensor_copy(kT[0:QK, 4 * g:4 * g + 4, t * P:(t + 1) * P], bank[4 + i][0:QK, :].rearrange("p (h s) -> p h s", s=P)).then_inc(kT_ready, 1)
            head_max(0)
            head_norm(0)
            conv(1)
            for h in range(HEADS):
                if h + 1 < HEADS:
                    head_max(h + 1)
                    head_norm(h + 1)
                if h in (3, 6):
                    conv(2 if h == 3 else 3)

            for d in range(KT):
                dve.wait_ge(sig_ready, d + 1)
                dve.wait_ge(y_mm, d + 1)
                g = gated[d % 2]
                link(dve.tensor_tensor(g, sig[d % 2], bank[2 * (d % 2) + 1][:, :].rearrange("p (g s) -> p g s", s=SEQ), mult))
                dve.tensor_tensor(mergedT[:, d, :], g[:, 0, :], g[:, 1, :], add).then_inc(merged, 1)
            for t in range(TT):
                for i in range(2):
                    dve.wait_ge(x1_mm, 2 * t + i + 1)
                    cols = slice(512 * i, 512 * i + 512)
                    last = dve.tensor_tensor(x_sb[:, t, cols], bank[4 + 2 * t + i][:, :], x_sb[:, t, cols], add)
                last.then_inc(x1_ready, 1)
                dve.wait_ge(x1_sq, t + 1)
                scaled(40 + t, 1, D)
                dve.wait_ge(rs_ready, 6 + t)
                dve.tensor_scalar(h_sb[:, t, :], x_sb[:, t, :], rs[:, 40 + t:41 + t], None, mult).then_inc(h2_ready, 1)
            for t in range(TT):
                for i in range(2):
                    dve.wait_ge(h2_tr, 2 * t + i + 1)
                    norm_out(t, i, G2, h2T_ready)
            dve.wait_ge(rb_in, 16)
            for t in range(TT):
                dve.wait_ge(logit_mm, t + 1)
                eight = slice(8 * t, 8 * t + 8)
                link(dve.tensor_tensor(logit[:, t, :], bank[4 + 2 * t][:, 0:EXPERTS], rb_sb[:, :], add))
                link(dve.max(top[:, eight], logit[:, t, :]))
                dve.tensor_scalar(ntop[:, t:t + 1], top[:, 8 * t:8 * t + 1], -1.0, None, mult).then_inc(ntop_ready, 1)
                link(dve.max_index(topi[:, eight], top[:, eight], logit[:, t, :]))
                link(dve.tensor_copy(topf[:, eight], topi[:, eight]))
                link(dve.tensor_scalar(mask[:, t, :], slots[:, 0:EXPERTS], topf[:, 8 * t:8 * t + 1], None, ALU.is_equal))
                for j in range(1, TOPK):
                    last = dve.scalar_tensor_tensor(mask[:, t, :], slots[:, 0:EXPERTS], topf[:, 8 * t + j:8 * t + j + 1], mask[:, t, :], ALU.is_equal, add)
                    if j < TOPK - 1:
                        link(last)
                last.then_inc(mask_ready, 1)
            dve.wait_ge(mask_ready, 2)
            for t in range(TT):
                dve.wait_ge(ew_ready, t + 1)
                last = dve.scalar_tensor_tensor(ew[:, t, :], ew[:, t, :], 1.0, mask[:, t, :], mult, mult, accum_out=esum[:, t:t + 1])
            link(last)
            link(dve.reciprocal(ersum[:, :], esum[:, :]))
            for t in range(TT):
                last = dve.tensor_scalar(wd[:, t, :], ew[:, t, :], ersum[:, t:t + 1], None, mult)
            last.then_inc(wd_ready, 1)
            dve.wait_ge(rank_mm, 1)
            link(dve.scalar_tensor_tensor(rank[:, :, 0:EXPERTS], bank[5][:, 0:2 * EXPERTS].rearrange("p (t e) -> p t e", t=TT), 1.0, mask, add, mult))
            dve.wait_ge(consts2, 1)
            link(dve.tensor_scalar(rank[:, :, 0:EXPERTS], rank[:, :, 0:EXPERTS], -1.0, None, add))

            def build_pick(col, signal):
                for t in range(TT):
                    last = dve.tensor_scalar(pick[:, t, :], slots[:, 0:CH], rank[:, t, col], None, ALU.is_equal)
                last.then_inc(signal, 1)

            def experts(c):
                first = c * (EXPERTS + 1)
                if not isinstance(c, int):
                    dve.tensor_scalar(rank[:, :, :], rank[:, :, :], -float(CH), None, add).then_inc(rank_moved, 1)
                    dve.wait_ge(rank_moved, c)
                build_pick(slice(0, 1), pick_ready)
                dve.tensor_scalar(sel, half_mask, one_hot[:, 0:1], None, mult).then_inc(sel_ready, 1)
                if isinstance(c, int):
                    link(dve.tensor_reduce(cmax[:, :], bank[5][:, 2 * EXPERTS:3 * EXPERTS], AX.X, ALU.max))
                    dve.tensor_copy(cmax_i[:, :], cmax[:, :]).then_inc(count_ready, 1)
                gather_out(first + 1)
                if isinstance(c, int):
                    for t, dsts in enumerate(((COMB0, COMB1), (CTP, ATP))):
                        dve.wait_ge(b2_mm, t + 1)
                        for i in range(2):
                            cols = slice(512 * i, 512 * i + 512)
                            last = dve.tensor_tensor(x_sb[:, t, cols], dsts[i][:, :], x_sb[:, t, cols], add)
                        last.then_inc(added, 1)
                with dve.Fori(0, EXPERTS) as e:
                    n = e + EXPERTS * c
                    build_pick(ds(e + 1, 1), pick_ready)
                    dve.wait_ge(bias_used, n + 1)
                    dve.tensor_scalar(sel, half_mask, one_hot[:, ds(e + 1, 1)], None, mult).then_inc(sel_ready, 1)
                    for t in range(TT):
                        last = dve.tensor_scalar(pick_w[:, t, :], slots[:, :], rank[:, t, ds(e, 1)], wd[:, t, ds(e, 1)], ALU.is_equal, mult)
                    last.then_inc(pickw_ready, 1)
                    dve.wait_ge(w1_used, n * KT + 2 * KT)
                    dve.tensor_scalar(gate_sb, GATE[:, :], LIMIT, None, ALU.min).then_inc(gate_ready, 1)
                    dve.tensor_scalar(up_sb, UP[:, :], LIMIT, -LIMIT, ALU.min, ALU.max).then_inc(up_ready, 1)
                    dve.wait_ge(up_ready, n + 1)
                    dve.scalar_tensor_tensor(up_sb, up_sb, 1.0, gate_sb, add, mult).then_inc(prod_ready, 1)
                    dve.wait_ge(prod_ready, n + 1)
                    dve.wait_ge(esig_ready, n + 1)
                    dve.tensor_tensor(up_sb, up_sb, sg_sb, mult).then_inc(act_ready, 1)
                    gather_out(first + e + 2)
                    dve.wait_ge(w2_used, n * KT + 2 * KT)
                    dve.tensor_copy(y_sb, YP[:, :]).then_inc(y_ready, 1)
                    for t, dsts in enumerate(((COMB0, COMB1), (CTP, ATP))):
                        dve.wait_ge(comb_mm, n * 2 + (t + 1))
                        for i in range(2):
                            cols = slice(512 * i, 512 * i + 512)
                            last = dve.tensor_tensor(x_sb[:, t, cols], dsts[i][:, :], x_sb[:, t, cols], add)
                        last.then_inc(added, 1)

            def gather_out(count):
                dve.wait_ge(gathered, count)
                dve.tensor_tensor(xT, XTP[:, :].rearrange("p (k s) -> p k s", s=CH), bc(parT[:, G2:G2 + 8].unsqueeze(2), P, KT, CH), mult).then_inc(xT_ready, 1)

            experts(0)
            dve.wait_ge(count_ready, 1)
            most = dve.value_load(cmax_i[0:1, 0:1], min_val=0, max_val=SEQ)
            with dve.If(most > CH):
                with dve.Fori(1, PASSES) as c:
                    with dve.If(most > c * CH):
                        experts(c)


_INS = ['x', 'positions', 'norm1_g', 'w_in', 'q_a_norm_g', 'kv_a_norm_g', 'w_uq', 'w_ukv', 'q_norm_g', 'k_norm_g',
        'conv_w', 'w_o_mla', 'w_o_conv', 'w_o', 'norm2_g', 'router_w', 'router_b', 'expert_w1', 'expert_b1',
        'expert_w2', 'expert_b2']


def kernel(**inputs):
    import numpy as _np
    import concourse.bacc as _bacc
    from concourse import mybir as _mybir
    from concourse.bass_utils import run_bass_kernel_spmd as _run

    nc = _bacc.Bacc("TRN2", target_bir_lowering=False, num_devices=1)
    arrays, args = {}, []
    for name in _INS:
        a = _np.ascontiguousarray(inputs[name])
        arrays[f"in_{name}"] = a
        args.append(nc.dram_tensor(f"in_{name}", a.shape, _mybir.dt.from_np(a.dtype), kind="ExternalInput").ap())
    args.append(nc.dram_tensor("out_x", (1, SEQ, D), _mybir.dt.float32, kind="ExternalOutput").ap())
    build(nc, *args)
    r = _run(nc, [arrays], core_ids=[0])
    return r.results[0]["out_x"]
```

```python
import concourse.bass as bass
from concourse import mybir
from contextlib import ExitStack
import numpy as np

D, SEQ, P = 1024, 256, 128
TT, KT = SEQ // P, D // P
HEADS, NOPE, ROPE, VH = 8, 64, 32, 64
QK = NOPE + ROPE
HR = ROPE // 2
QL, KVL, CW = 256, 128, 512
A_COLS = QL + KVL + ROPE
CT = CW // P
EXPERTS, TOPK, FF = 32, 4, 1024
CH = 64
PASSES = SEQ // CH
PAIRS = EXPERTS // 2
KVX = NOPE + ROPE + VH
SMALL = 2793
EPS = 1e-6
THETA = 10000.0
LIMIT, ALPHA = 7.0, 1.702


def build(nc, x, positions, norm1_g, w_in, q_a_norm_g, kv_a_norm_g, w_uq, w_ukv, q_norm_g, k_norm_g,
          conv_w, w_o_mla, w_o_conv, w_o, norm2_g, router_w, router_b, expert_w1, expert_b1,
          expert_w2, expert_b2, out):
    fp32, i32, u32 = mybir.dt.float32, mybir.dt.int32, mybir.dt.uint32
    ALU, ACT, AX = mybir.AluOpType, mybir.ActivationFunctionType, mybir.AxisListType
    ds = bass.ds

    ctx = ExitStack()
    with ctx:
        def sb(name, cols, dt=fp32, rows=P):
            return ctx.enter_context(nc.sbuf_tensor(name, [rows, cols], dt))

        def sem(name):
            return ctx.enter_context(nc.semaphore(name))

        def view(region, at, *shape, rows=P):
            n = int(np.prod(shape))
            part = region[0:rows, at:at + n]
            if len(shape) == 1:
                return part
            names = "abc"[:len(shape)]
            text = f"p ({' '.join(names)}) -> p {' '.join(names)}"
            return part.rearrange(text, **{c: s for c, s in zip(names[1:], shape[1:])})

        W1 = sb("W1", KT * 2 * FF)
        W2 = sb("W2", KT * D)
        W1B = sb("W1B", KT * 2 * FF + SMALL)
        WA, ATT = W1B[:, 0:9984], W1B[:, 9984:9984 + 9024]
        SM = W1B[:, KT * 2 * FF:]
        X = sb("X", TT * D)
        H = sb("H", TT * D)
        HT = sb("HT", KT * SEQ)
        OT = sb("OT", 1024)
        YB = sb("YB", 1024)

        w1_sb = view(W1, 0, KT, 2 * FF)
        w2_sb = view(W2, 0, KT, D)
        w_gates = [view(W1, i * 4096, KT, 2, 2 * P) for i in range(KT // 2)]
        w_o_sb = view(W1, 0, KT, D)
        w_uc = w2_sb
        w_mla = view(W2, 0, CT, D)
        w_cnv = view(W2, CT * D, CT, D)
        w_a = view(WA, 0, KT, A_COLS)
        w_uq_sb = view(WA, 3328, 2, HEADS * QK)
        w_ukv_sb = WA[:, 4864:5888]
        w_b = view(WA, 5888, KT, CW)
        cu = [view(WA, i * 258, 258) for i in range(2)]
        c_sb = [view(WA, 520 + i * 256, 256) for i in range(2)]
        y_tmp = [view(WA, 1032 + i * 256, 256) for i in range(2)]
        krot = WA[:, 2832:2832 + TT * ROPE]
        mx, nm, sums, rsum = (WA[:, 2896 + i * 16:2912 + i * 16] for i in range(4))
        rot_tmp = [view(WA, 1600 + i * 256, TT, HEADS, HR) for i in range(4)]
        krot_tmp = [view(WA, 2640 + i * 32, TT, HR) for i in range(4)]

        x_sb = view(X, 0, TT, D)
        h_sb = view(H, 0, TT, D)
        sq_a = [H[:, 1536:1536 + A_COLS], YB[:, 512:512 + A_COLS]]
        sq_q = [view(H, 768 * t, HEADS, QK) for t in range(TT)]
        sq_k = [view(YB, 512 * t, HEADS, NOPE) for t in range(TT)]
        prob = [view(H, 512 * i, TT, SEQ) for i in range(2)]
        prob_t = [view(H, 1024 + 512 * i, TT, SEQ) for i in range(2)]
        sig = [view(H, 512 * i, 2, SEQ) for i in range(2)]
        gated = [view(H, 1024 + 512 * i, 2, SEQ) for i in range(2)]
        hT = view(HT, 0, KT, SEQ)

        q_sb = view(ATT, 0, TT, HEADS, QK)
        kvx = view(ATT, 1536, TT, HEADS, KVX)
        qT = view(ATT, 4096, HEADS, SEQ)
        kT = view(ATT, 6144, HEADS, SEQ)
        lat = view(ATT, 8192, TT, QL + KVL)
        krg = view(ATT, 8960, TT, ROPE)
        latT = view(OT, 0, 3, SEQ)
        oT = view(OT, 0, CT, SEQ)
        yT = view(YB, 0, CT, SEQ)
        rope_t = [view(YB, 32 * i, TT, HR) for i in range(8)]

        mergedT = view(W1B, (KT - 1) * 2 * FF, KT, SEQ)
        w1b_sb = view(W1B, 0, KT, 2 * FF)
        w1_of = (w1b_sb, w1_sb)
        xT = view(HT, 0, KT, P)
        gate_sb, up_sb = HT[:, 1024:1536], HT[:, 1536:2048]
        sg_sb = YB[:, 0:512]
        comb = view(YB, 512, TT, P)
        pick_w = view(YB, 768, TT, P)
        y_sb = view(OT, 0, 2, 512)
        b1_sb = view(SM, 0, 2, 512, rows=2 * EXPERTS)
        b2_sb = SM[0:2 * EXPERTS, 1024:1536]
        rw_sb = view(SM, 1536, KT, EXPERTS)
        actT = view(SM, 1536, 4, P)
        pick = view(SM, 2048, TT, P)
        sel = [SM[0:2 * EXPERTS, 2304 + P * i:2304 + P * (i + 1)] for i in range(2)]
        half_mask = SM[0:2 * EXPERTS, 2560:2688]
        rank = view(SM, 2688, TT, EXPERTS + 2)
        one_hot = SM[0:2 * EXPERTS, 2756:2756 + EXPERTS + 2]
        logit = view(OT, 0, TT, EXPERTS)
        mask = view(OT, 64, TT, EXPERTS)
        ew = view(OT, 128, TT, EXPERTS)
        first4 = view(OT, 192, TOPK, EXPERTS)
        top = OT[:, 320:336]
        topi = OT[:, 336:352].bitcast(u32)
        ntop, esum, ersum = (OT[:, 352 + TT * i:354 + TT * i] for i in range(3))
        wd_sb = sb("wd", TT * EXPERTS)
        ident = sb("ident", P)
        wd = wd_sb[:, :].rearrange("p (t e) -> p t e", t=TT)
        before = sb("before", P)
        ones = sb("ones", P)
        slots = sb("slots", CH)
        expert_no = sb("expert_no", TOPK * EXPERTS)
        qg_sb, kg_sb = sb("qg_sb", QK), sb("kg_sb", QK)
        rb_sb = sb("rb_sb", EXPERTS)
        par = ATT[0:32, 0:P]
        pos_i = ATT[0:TT, P:2 * P].bitcast(i32)
        pos_f = ATT[0:TT, 2 * P:3 * P]
        parT = sb("parT", 34)
        invf = sb("invf", HR)
        mhalf = sb("mhalf", 32)
        cos_sb, sin_sb = sb("cos_sb", TT * HR), sb("sin_sb", TT * HR)
        ss, ms, rs = sb("ss", 48), sb("ms", 48), sb("rs", 48)
        rq = sb("rq", 16)
        cmax = sb("cmax", 1)
        cmax_i = sb("cmax_i", 1, i32)

        G1, G2, GL, GC = 0, 8, 16, 19

        bank = [ctx.enter_context(nc.psum_tensor(f"bank{i}", [P, 512], fp32)) for i in range(8)]
        GATE, UP, XTP0, XTP1, CTP, ATP, YP, CMB = bank

        x_in = [sem(f"x_in{t}") for t in range(TT)]
        par_in, pos_in, gains_in, rb_in = sem("par_in"), sem("pos_in"), sem("gains_in"), sem("rb_in")
        wa_in = [sem(f"wa_in{i}") for i in range(2)]
        uq_in, ukv_in, b_in = sem("uq_in"), sem("ukv_in"), sem("b_in")
        uc_in = [sem(f"uc_in{i}") for i in range(2)]
        gates_in = [sem(f"gates_in{i}") for i in range(4)]
        mla_in, cnv_in = sem("mla_in"), sem("cnv_in")
        wo_in = [sem(f"wo_in{i}") for i in range(2)]
        router_in, b1_in, b2_in = sem("router_in"), sem("b1_in"), sem("b2_in")
        w1_in = [[sem(f"w1{'ab'[a]}_in{k}") for k in range(KT)] for a in range(2)]
        w2_in = [sem(f"w2_in{k}") for k in range(KT)]
        stored = [sem(f"stored{t}") for t in range(TT)]
        consts, consts2 = sem("consts"), sem("consts2")
        pool_step, dve_step = sem("pool_step"), sem("dve_step")
        pos_ready, par_tr, x_sq, ms_ready, rs_ready = (sem(n) for n in ("pos_ready", "par_tr", "x_sq", "ms_ready", "rs_ready"))
        h_ready, h_tr, hT_ready = sem("h_ready"), sem("h_tr"), sem("hT_ready")
        lat_mm, lat_sq, lat_ready, lat_tr, latT_ready = (sem(n) for n in ("lat_mm", "lat_sq", "lat_ready", "lat_tr", "latT_ready"))
        q_mm, kv_mm, q_sq, k_sq, q_out, k_out, v_out = (sem(n) for n in ("q_mm", "kv_mm", "q_sq", "k_sq", "q_out", "k_out", "v_out"))
        rope_ready = sem("rope_ready")
        q_ready, k_ready, q_tr, k_tr, qT_ready, kT_ready = (sem(n) for n in ("q_ready", "k_ready", "q_tr", "k_tr", "qT_ready", "kT_ready"))
        uc_mm, b_mm, c_out, yT_ready = sem("uc_mm"), sem("b_mm"), sem("c_out"), sem("yT_ready")
        s_mm, max_ready, exp_ready, p_norm, p_tr, pT_ready, o_mm, oT_ready = (
            sem(n) for n in ("s_mm", "max_ready", "exp_ready", "p_norm", "p_tr", "pT_ready", "o_mm", "oT_ready"))
        gate_mm, y_mm, sig_ready, merged = sem("gate_mm"), sem("y_mm"), sem("sig_ready"), sem("merged")
        x1_mm, x1_ready, x1_sq, h2_ready, x1_tr, x1T_ready = (
            sem(n) for n in ("x1_mm", "x1_ready", "x1_sq", "h2_ready", "x1_tr", "x1T_ready"))
        logit_mm, ntop_ready, ew_ready, mask_ready, rank_mm, count_ready = (
            sem(n) for n in ("logit_mm", "ntop_ready", "ew_ready", "mask_ready", "rank_mm", "count_ready"))
        pick_ready, sel_ready, pickw_ready = sem("pick_ready"), sem("sel_ready"), sem("pickw_ready")
        gathered, xT_ready, w2_used = (sem(n) for n in ("gathered", "xT_ready", "w2_used"))
        w1_used = [sem("w1a_used"), sem("w1b_used")]
        gate_ready, up_ready, esig_ready, prod_ready, act_ready = (
            sem(n) for n in ("gate_ready", "up_ready", "esig_ready", "prod_ready", "act_ready"))
        pass_stored, rank_moved, pickw_tr, comb_ready, act_tr, actT_ready, y_low, y_high, comb_mm, added = (
            sem(n) for n in ("pass_stored", "rank_moved", "pickw_tr", "comb_ready", "act_tr", "actT_ready", "y_low", "y_high", "comb_mm", "added"))

        block = ctx.enter_context(nc.Block())

        def rows(w):
            return w.rearrange("(k p) n -> p k n", p=P)

        @block.sync
        def _(sp):
            for t in range(TT):
                sp.dma_start(x_sb[:, t, :], x[0, t * P:(t + 1) * P, :]).then_inc(x_in[t], 16)
            sp.dma_start(pos_i[:, :], positions[0].rearrange("(t p) -> t p", p=P)).then_inc(pos_in, 16)
            sp.dma_start(par[G1:G1 + 8, :], norm1_g[0].rearrange("(k p) -> k p", p=P)).then_inc(par_in, 16)
            sp.dma_start(par[G2:G2 + 8, :], norm2_g[0].rearrange("(k p) -> k p", p=P)).then_inc(par_in, 16)
            sp.dma_start(par[GL:GL + 2, :], q_a_norm_g[0].rearrange("(k p) -> k p", p=P)).then_inc(par_in, 16)
            sp.dma_start(par[GL + 2:GL + 3, :], kv_a_norm_g[0].rearrange("(k p) -> k p", p=P)).then_inc(par_in, 16)
            sp.dma_start(par[GC:GC + 12, :], conv_w[0].rearrange("w (k p) -> (w k) p", p=P)).then_inc(par_in, 16)
            wi = rows(w_in[0])
            for i in range(2):
                sp.dma_start(w_a[:, 4 * i:4 * i + 4, :], wi[:, 4 * i:4 * i + 4, 0:A_COLS]).then_inc(wa_in[i], 16)
            sp.dma_start(w_uq_sb, rows(w_uq[0])).then_inc(uq_in, 16)
            sp.dma_start(w_ukv_sb, w_ukv[0]).then_inc(ukv_in, 16)
            for i in range(2):
                sp.dma_start(w_uc[:, 4 * i:4 * i + 4, :],
                             wi[:, 4 * i:4 * i + 4, A_COLS:A_COLS + 2 * CW]).then_inc(uc_in[i], 16)
            sp.dma_start(w_b, wi[:, :, A_COLS + 2 * CW:A_COLS + 3 * CW]).then_inc(b_in, 16)
            for i in range(KT // 2):
                for g in range(2):
                    at = A_COLS + 3 * CW + g * D + i * 2 * P
                    sp.dma_start(w_gates[i][:, :, g, :], wi[:, :, at:at + 2 * P]).then_inc(gates_in[i], 16)
            sp.wait_ge(uc_mm, CT)
            sp.dma_start(w_mla, rows(w_o_mla[0])).then_inc(mla_in, 16)
            sp.dma_start(w_cnv, rows(w_o_conv[0])).then_inc(cnv_in, 16)
            sp.wait_ge(yT_ready, CT)
            sp.wait_ge(o_mm, HEADS)
            sp.dma_start(rw_sb, rows(router_w[0])).then_inc(router_in, 16)
            for i in range(2):
                sp.dma_start(b1_sb[i * EXPERTS:(i + 1) * EXPERTS, :, :],
                             expert_b1[0].rearrange("e (s h n) -> e s h n", s=2, h=2)[:, :, i, :]).then_inc(b1_in, 16)
                sp.dma_start(b2_sb[i * EXPERTS:(i + 1) * EXPERTS, :],
                             expert_b2[0].rearrange("e (h n) -> e h n", h=2)[:, i, :]).then_inc(b2_in, 16)

            def load_experts(c):
                def load_w1(j, a, tiles=range(KT), free=False):
                    for k in tiles:
                        if not free:
                            sp.wait_ge(w1_used[a], (j + PAIRS * c) * KT + (k + 1))
                        sp.dma_start(w1_of[a][:, k, :], expert_w1[0, ds(j * 2 + a, 1), k * P:(k + 1) * P, :].rearrange("a p n -> p (a n)")).then_inc(w1_in[a][k], 16)

                def load_w2(j, a):
                    for k in range(KT):
                        sp.wait_ge(w2_used, (j + PAIRS * c) * (2 * KT) + (a * KT + k + 1))
                        sp.dma_start(w2_sb[:, k, :], expert_w2[0, ds(j * 2 + a, 1), k * P:(k + 1) * P, :].rearrange("a p n -> p (a n)")).then_inc(w2_in[k], 16)

                if isinstance(c, int):
                    load_w1(0, 0, range(KT - 1), free=True)
                    sp.wait_ge(gate_mm, KT // 2)
                    for i in range(2):
                        sp.dma_start(w_o_sb[:, 4 * i:4 * i + 4, :], rows(w_o[0])[:, 4 * i:4 * i + 4, :]).then_inc(wo_in[i], 16)
                    sp.wait_ge(w1_used[1], KT // 2)
                    load_w1(0, 1, range(KT // 2, KT), free=True)
                    load_w2(0, 0)
                    sp.wait_ge(w1_used[0], KT)
                    load_w1(0, 0, [KT - 1], free=True)
                    sp.wait_ge(w1_used[1], KT)
                    load_w1(0, 1, range(KT // 2), free=True)
                else:
                    load_w1(0, 0)
                    load_w2(0, 0)
                    load_w1(0, 1)
                load_w1(1, 0)
                load_w1(1, 1)
                load_w2(0, 1)
                load_w2(1, 0)
                with sp.Fori(0, PAIRS - 2) as j:
                    load_w1(j + 2, 0)
                    load_w2(j + 1, 1)
                    load_w1(j + 2, 1)
                    load_w2(j + 2, 0)
                load_w2(PAIRS - 1, 1)

            load_experts(0)
            sp.wait_ge(count_ready, 1)
            most = sp.value_load(cmax_i[0:1, 0:1], min_val=0, max_val=SEQ)
            with sp.If(most > CH):
                with sp.Fori(1, PASSES) as c:
                    with sp.If(most > c * CH):
                        load_experts(c)
                        sp.wait_ge(added, c * (2 * PAIRS) + (2 * PAIRS + 2))
                        sp.sem_inc(pass_stored, 1)
            for t in range(TT):
                sp.wait_ge(added, 2 * PAIRS + 1 + t)
                sp.dma_start(out[0, t * P:(t + 1) * P, :], x_sb[:, t, :]).then_inc(stored[t], 16)
            for t in range(TT):
                sp.wait_ge(stored[t], 16)

        @block.gpsimd
        def _(pool):
            n = [0]

            def link(ins):
                n[0] += 1
                ins.then_inc(pool_step, 1)
                pool.wait_ge(pool_step, n[0])

            pool.memset(ident[:, :], 0.0)
            link(pool.memset(before[:, :], 1.0))
            pool.affine_select(out=ident[:, :], in_=ident[:, :], compare_op=ALU.not_equal, fill=1.0,
                               base=0, pattern=[[-1, P]], channel_multiplier=1).then_inc(consts, 1)
            pool.memset(mhalf[:, :], -0.5)
            inv = np.float32(THETA) ** (-np.arange(0, ROPE, 2, dtype=np.float32) / np.float32(ROPE))
            for i in range(HR):
                last = pool.memset(invf[:, i:i + 1], float(inv[i]))
            link(last)
            pool.affine_select(out=before[:, :], in_=before[:, :], compare_op=ALU.is_gt, fill=0.0,
                               base=0, pattern=[[1, P]], channel_multiplier=-1)
            pool.memset(ones[:, :], 1.0)
            pool.iota(slots[:, :], pattern=[[1, CH]], base=1, channel_multiplier=0,
                      allow_small_or_imprecise_dtypes=True)
            pool.iota(expert_no[:, :], pattern=[[0, TOPK], [1, EXPERTS]], base=0, channel_multiplier=0,
                      allow_small_or_imprecise_dtypes=True).then_inc(consts, 1)
            pool.dma_start(qg_sb[:, :], q_norm_g[0].partition_broadcast(P)).then_inc(gains_in, 16)
            pool.dma_start(kg_sb[:, :], k_norm_g[0].partition_broadcast(P)).then_inc(gains_in, 16)
            pool.dma_start(rb_sb[:, :], router_b[0].partition_broadcast(P)).then_inc(rb_in, 16)

            def power(at, width, k):
                pool.wait_ge(ms_ready, k)
                pool.tensor_tensor(rs[:, at:at + width], ms[:, at:at + width], mhalf[:, 0:width],
                                   ALU.pow).then_inc(rs_ready, 1)

            for t in range(TT):
                power(t, 1, 1 + t)
            for t in range(TT):
                power(2 + 2 * t, 2, 3 + t)
            power(8, 32, 5)
            pool.wait_ge(o_mm, HEADS)
            link(pool.memset(rank[:, :, EXPERTS:], -1.0))
            for i in range(2):
                rows_i = slice(i * EXPERTS, (i + 1) * EXPERTS)
                link(pool.memset(half_mask[rows_i, i * CH:(i + 1) * CH], 1.0))
                link(pool.memset(half_mask[rows_i, (1 - i) * CH:(2 - i) * CH], 0.0))
            link(pool.memset(one_hot, 0.0))
            for i in range(2):
                part = one_hot[i * EXPERTS:(i + 1) * EXPERTS, :]
                link(pool.affine_select(out=part, in_=part, compare_op=ALU.not_equal, fill=1.0,
                                        base=0, pattern=[[-1, EXPERTS + 2]], channel_multiplier=1))
            pool.sem_inc(consts2, 1)
            for t in range(TT):
                power(40 + t, 1, 6 + t)

        @block.scalar
        def _(act):
            for t in range(TT):
                act.wait_ge(x_in[t], 16)
                act.activation(HT[:, t * D:(t + 1) * D], x_sb[:, t, :], ACT.Square,
                               accum_out=ss[:, t:t + 1]).then_inc(x_sq, 1)
            for t in range(TT):
                act.wait_ge(lat_mm, t + 1)
                for a, b, col in ((0, QL, 2 + 2 * t), (QL, QL + KVL, 3 + 2 * t), (QL + KVL, A_COLS, 6 + t)):
                    last = act.activation(sq_a[t][:, a:b], bank[4 + 2 * t][:, a:b], ACT.Square, accum_out=ss[:, col:col + 1])
                last.then_inc(lat_sq, 1)
            for t in range(TT):
                act.wait_ge(q_mm, t + 1)
                for i in range(2):
                    last = act.activation(sq_q[t][:, 4 * i:4 * i + 4, :],
                                          bank[2 * t + i][:, 0:4 * QK].rearrange("p (h d) -> p h d", d=QK), ACT.Square)
                last.then_inc(q_sq, 1)
            for t in range(TT):
                act.wait_ge(kv_mm, t + 1)
                for i in range(2):
                    kv = bank[4 + 2 * t + i][:, :].rearrange("p (h d) -> p h d", d=NOPE + VH)
                    last = act.activation(sq_k[t][:, 4 * i:4 * i + 4, :], kv[:, :, 0:NOPE], ACT.Square)
                last.then_inc(k_sq, 1)
                for i in range(2):
                    kv = bank[4 + 2 * t + i][:, :].rearrange("p (h d) -> p h d", d=NOPE + VH)
                    last = act.activation(kvx[:, t, 4 * i:4 * i + 4, QK:KVX], kv[:, :, NOPE:], ACT.Copy)
                last.then_inc(v_out, 1)

            def conv_c(f):
                act.wait_ge(uc_mm, f + 1)
                if f >= 2:
                    act.wait_ge(yT_ready, f - 1)
                act.activation(c_sb[f % 2], bank[2 * (f % 2)][:, SEQ:2 * SEQ], ACT.Copy).then_inc(c_out, 1)

            conv_c(0)
            for i in range(4):
                t, g = i // 2, i % 2
                act.wait_ge(q_tr, i + 1)
                act.activation(qT[0:QK, 4 * g:4 * g + 4, t * P:(t + 1) * P],
                               bank[4 + i][0:QK, :].rearrange("p (h s) -> p h s", s=P), ACT.Copy).then_inc(qT_ready, 1)

            def head_exp(h):
                act.wait_ge(max_ready, h + 1)
                if h >= 2:
                    act.wait_ge(p_tr, h - 1)
                for t in range(TT):
                    c = TT * h + t
                    last = act.activation(prob[h % 2][:, t, :], bank[4 + h % 2][:, t * SEQ:(t + 1) * SEQ], ACT.Exp,
                                          bias=nm[:, c:c + 1], scale=rq[:, c:c + 1], accum_out=sums[:, c:c + 1])
                last.then_inc(exp_ready, 1)

            def head_pair_out(i):
                act.wait_ge(o_mm, 2 * i + 2)
                act.activation(oT[:, i, :], bank[7][:, 0:SEQ], ACT.Copy).then_inc(oT_ready, 1)

            head_exp(0)
            conv_c(1)
            for h in range(HEADS):
                if h + 1 < HEADS:
                    head_exp(h + 1)
                act.wait_ge(p_tr, h + 1)
                act.activation(prob_t[h % 2], bank[6][:, :].rearrange("p (k s) -> p k s", s=SEQ), ACT.Copy).then_inc(pT_ready, 1)
                if h % 2 == 0 and h:
                    head_pair_out(h // 2 - 1)
                if h in (3, 6):
                    conv_c(2 if h == 3 else 3)
            head_pair_out(HEADS // 2 - 1)
            for d in range(KT):
                act.wait_ge(gate_mm, d + 1)
                if d >= 2:
                    act.wait_ge(merged, d - 1)
                act.activation(sig[d % 2], bank[2 * (d % 2)][:, :].rearrange("p (g s) -> p g s", s=SEQ), ACT.Sigmoid).then_inc(sig_ready, 1)
            for t in range(TT):
                for i in range(2):
                    act.wait_ge(x1_ready, 2 * t + i + 1)
                    last = act.activation(h_sb[:, t, 512 * i:512 * i + 512], x_sb[:, t, 512 * i:512 * i + 512], ACT.Square, accum_out=ss[:, 40 + 2 * t + i:41 + 2 * t + i])
                last.then_inc(x1_sq, 1)
                act.wait_ge(rs_ready, 6 + t)
                act.activation(h_sb[:, t, :], x_sb[:, t, :], ACT.Copy, scale=rs[:, 40 + t:41 + t]).then_inc(h2_ready, 1)
            for t in range(TT):
                act.wait_ge(ntop_ready, t + 1)
                act.activation(ew[:, t, :], logit[:, t, :], ACT.Exp, bias=ntop[:, t:t + 1]).then_inc(ew_ready, 1)

            def sigmoid(e):
                act.wait_ge(gate_ready, e + 1)
                act.activation(sg_sb, gate_sb, ACT.Sigmoid, scale=ALPHA).then_inc(esig_ready, 1)

            def expert_out(e, a):
                act.wait_ge(act_tr, e + 1)
                act.activation(actT, ATP[:, :].rearrange("p (j s) -> p j s", s=P), ACT.Copy).then_inc(actT_ready, 1)
                act.wait_ge(w2_used, e * KT + 2 * KT)
                act.activation(y_sb[a * CH:(a + 1) * CH, 1, :], YP[CH:P, :], ACT.Copy).then_inc(y_high, 1)

            def two_experts(j, c, last):
                pair = j + PAIRS * c
                sigmoid(pair * 2 + 1)
                expert_out(pair * 2, 0)
                if not last:
                    sigmoid(pair * 2 + 2)
                act.wait_ge(pickw_tr, pair + 1)
                act.activation(comb, CTP[:, 0:SEQ].rearrange("p (t s) -> p t s", s=P), ACT.Copy).then_inc(comb_ready, 1)
                expert_out(pair * 2 + 1, 1)

            def experts(c):
                sigmoid(c * EXPERTS)
                with act.Fori(0, PAIRS - 1) as j:
                    two_experts(j, c, False)
                two_experts(PAIRS - 1, c, True)

            experts(0)
            act.wait_ge(count_ready, 1)
            most = act.value_load(cmax_i[0:1, 0:1], min_val=0, max_val=SEQ)
            with act.If(most > CH):
                with act.Fori(1, PASSES) as c:
                    with act.If(most > c * CH):
                        experts(c)

        @block.tensor
        def _(pe):
            pe.wait_ge(consts, 1)
            pe.wait_ge(par_in, 80)
            pe.wait_ge(pos_ready, 1)
            pe.transpose(bank[7][:, 0:31], par[0:31, :], ident[0:31, 0:31])
            pe.transpose(bank[7][:, 32:34], pos_f[:, :], ident[0:TT, 0:TT]).then_inc(par_tr, 1)
            for t in range(TT):
                pe.wait_ge(h_ready, t + 1)
                for k in range(KT):
                    last = pe.transpose(bank[2 * t + k // 4][:, (k % 4) * P:(k % 4 + 1) * P], h_sb[:, t, k * P:(k + 1) * P], ident[:, :])
                    if k % 4 == 3:
                        last.then_inc(h_tr, 1)
            for t in range(TT):
                pe.wait_ge(hT_ready, 2 * t + 2)
                for k in range(KT):
                    pe.wait_ge(wa_in[k // 4], 16)
                    last = pe.matmul(bank[4 + 2 * t][:, 0:A_COLS], hT[:, k, t * P:(t + 1) * P], w_a[:, k, :], start=(k == 0), stop=(k == KT - 1))
                last.then_inc(lat_mm, 1)
            for t in range(TT):
                pe.wait_ge(lat_ready, t + 1)
                for k in range(3):
                    last = pe.transpose(bank[5 + 2 * t][:, k * P:(k + 1) * P], lat[:, t, k * P:(k + 1) * P], ident[:, :])
                last.then_inc(lat_tr, 1)
                pe.wait_ge(latT_ready, t + 1)
                pe.wait_ge(uq_in, 16)
                for i in range(2):
                    for k in range(2):
                        last = pe.matmul(bank[2 * t + i][:, 0:4 * QK], latT[:, k, t * P:(t + 1) * P],
                                         w_uq_sb[:, k, i * 4 * QK:(i + 1) * 4 * QK], start=(k == 0), stop=(k == 1))
                last.then_inc(q_mm, 1)
                pe.wait_ge(ukv_in, 16)
                for i in range(2):
                    last = pe.matmul(bank[4 + 2 * t + i][:, :], latT[:, 2, t * P:(t + 1) * P], w_ukv_sb[:, 512 * i:512 * i + 512], start=True, stop=True)
                last.then_inc(kv_mm, 1)

            def conv_group(i):
                f, part = divmod(i, 3)
                pair = 2 * (f % 2)
                if part == 0:
                    if f < 2:
                        pe.wait_ge(q_out, f + 1)
                        pe.wait_ge(q_sq, f + 1)
                    else:
                        pe.wait_ge(yT_ready, f - 1)
                dst = bank[pair + part // 2][:, (part % 2) * SEQ:(part % 2 + 1) * SEQ]
                for k in range(KT):
                    if part == 2:
                        pe.wait_ge(b_in, 16)
                        w = w_b[:, k, f * P:(f + 1) * P]
                    else:
                        pe.wait_ge(uc_in[k // 4], 16)
                        w = w_uc[:, k, part * CW + f * P:part * CW + (f + 1) * P]
                    last = pe.matmul(dst, w, hT[:, k, :], start=(k == 0), stop=(k == KT - 1))
                if part == 1:
                    last.then_inc(uc_mm, 1)
                elif part == 2:
                    last.then_inc(b_mm, 1)

            def head_scores(h):
                if h >= 2:
                    pe.wait_ge(exp_ready, h - 1)
                for t in range(TT):
                    last = pe.matmul(bank[4 + h % 2][:, t * SEQ:(t + 1) * SEQ], qT[0:QK, h, t * P:(t + 1) * P], kT[0:QK, h, :], start=True, stop=True)
                last.then_inc(s_mm, 1)

            def head_out(h):
                pe.wait_ge(pT_ready, h + 1)
                if h >= 2 and h % 2 == 0:
                    pe.wait_ge(oT_ready, h // 2)
                for k in range(TT):
                    last = pe.matmul(bank[7][VH * (h % 2):VH * (h % 2) + VH, 0:SEQ], kvx[:, k, h, QK:KVX], prob_t[h % 2][:, k, :], start=(k == 0), stop=(k == TT - 1))
                last.then_inc(o_mm, 1)

            for i in range(4):
                conv_group(i)
            pe.wait_ge(q_ready, 1)
            pe.wait_ge(k_out, 2)
            pe.wait_ge(v_out, 2)
            for i in range(4):
                t, g = i // 2, i % 2
                for h in range(4):
                    last = pe.transpose(bank[4 + i][0:QK, h * P:(h + 1) * P], q_sb[:, t, 4 * g + h, :], ident[:, :])
                last.then_inc(q_tr, 1)
            conv_group(4)
            pe.wait_ge(k_ready, 1)
            for i in range(4):
                t, g = i // 2, i % 2
                pe.wait_ge(qT_ready, i + 1)
                for h in range(4):
                    last = pe.transpose(bank[4 + i][0:QK, h * P:(h + 1) * P], kvx[:, t, 4 * g + h, 0:QK], ident[:, :])
                last.then_inc(k_tr, 1)
            conv_group(5)
            pe.wait_ge(kT_ready, 4)
            head_scores(0)
            for h in range(HEADS):
                if h + 1 < HEADS:
                    head_scores(h + 1)
                if h < 6:
                    conv_group(6 + h)
                pe.wait_ge(p_norm, h + 1)
                if h >= 1:
                    pe.wait_ge(pT_ready, h)
                for t in range(TT):
                    for k in range(TT):
                        last = pe.transpose(bank[6][:, k * SEQ + t * P:k * SEQ + (t + 1) * P], prob[h % 2][:, t, k * P:(k + 1) * P], ident[:, :])
                last.then_inc(p_tr, 1)
                if h >= 1:
                    head_out(h - 1)
            head_out(HEADS - 1)

            def gates(d):
                if d < 2:
                    pe.wait_ge(yT_ready, d + 3)
                else:
                    pe.wait_ge(sig_ready, d - 1)
                for g in range(2):
                    for k in range(KT):
                        pe.wait_ge(gates_in[d // 2], 32)
                        last = pe.matmul(bank[2 * (d % 2)][:, g * SEQ:(g + 1) * SEQ], w_gates[d // 2][:, k, g, (d % 2) * P:(d % 2 + 1) * P], hT[:, k, :], start=(k == 0), stop=(k == KT - 1))
                last.then_inc(gate_mm, 1)

            def branches(d):
                if d >= 2:
                    pe.wait_ge(merged, d - 1)
                pe.wait_ge(oT_ready, CT)
                pe.wait_ge(yT_ready, CT)
                pe.wait_ge(mla_in, 16)
                pe.wait_ge(cnv_in, 16)
                for g, (w, v) in enumerate(((w_mla, oT), (w_cnv, yT))):
                    for k in range(CT):
                        last = pe.matmul(bank[2 * (d % 2) + 1][:, g * SEQ:(g + 1) * SEQ], w[:, k, d * P:(d + 1) * P], v[:, k, :], start=(k == 0), stop=(k == CT - 1))
                        if d == KT - 2 and g == 0 and k == 0:
                            last.then_inc(w1_used[1], KT // 2)
                last.then_inc(y_mm, 1)

            gates(0)
            for d in range(KT):
                if d + 1 < KT:
                    gates(d + 1)
                branches(d)

            def x1_part(t, i, tiles):
                for k in tiles:
                    if t == 0 and i == 0:
                        pe.wait_ge(merged, k + 1)
                        pe.wait_ge(wo_in[k // 4], 16)
                    last = pe.matmul(bank[4 + 2 * t + i][:, :], mergedT[:, k, t * P:(t + 1) * P], w_o_sb[:, k, 512 * i:512 * i + 512], start=(k == 0), stop=(k == KT - 1))
                    if t == 0 and i == 0 and k == 0:
                        last.then_inc(w2_used, KT)
                    if k == KT - 1:
                        last.then_inc(x1_mm, 1)

            def x1_transposes(t, i):
                pe.wait_ge(x1_ready, 2 * t + i + 1)
                for k in range(4):
                    last = pe.transpose(bank[2 * t + i][:, k * P:(k + 1) * P], x_sb[:, t, (4 * i + k) * P:(4 * i + k + 1) * P], ident[:, :])
                last.then_inc(x1_tr, 1)

            def logits(t):
                for k in range(KT):
                    pe.wait_ge(x1T_ready, 2 * t + k // 4 + 1)
                    last = pe.matmul(bank[4 + 2 * t][:, 0:EXPERTS], hT[:, k, t * P:(t + 1) * P], rw_sb[:, k, :], start=(k == 0), stop=(k == KT - 1))
                last.then_inc(logit_mm, 1)

            x1_part(0, 0, range(KT))
            x1_part(0, 1, range(KT))
            x1_part(1, 0, range(KT))
            x1_transposes(0, 0)
            x1_transposes(0, 1)
            x1_part(1, 1, range(KT // 2))
            pe.wait_ge(router_in, 16)
            logits(0)
            x1_transposes(1, 0)
            x1_part(1, 1, range(KT // 2, KT))
            pe.wait_ge(x1_ready, 4)
            for k in range(4):
                last = pe.transpose(bank[3][:, k * P:(k + 1) * P], x_sb[:, 1, (4 + k) * P:(5 + k) * P], ident[:, :])
                if k == 0:
                    last.then_inc(w1_used[0], KT)
                elif k == 1:
                    last.then_inc(w1_used[1], KT // 2)
            last.then_inc(x1_tr, 1)
            logits(1)
            def bias(s, a):
                pe.matmul((GATE, UP)[s][:, :], sel[a], b1_sb[:, s, :], start=True, stop=True)

            def gather(count):
                pe.wait_ge(pick_ready, count)
                for k in range(KT):
                    dst = (XTP0, XTP1)[k // 4][:, (k % 4) * P:(k % 4 + 1) * P]
                    for t in range(TT):
                        last = pe.matmul(dst, h_sb[:, t, k * P:(k + 1) * P], pick[:, t, :], start=(t == 0), stop=(t == TT - 1))
                    if k % 4 == 3:
                        last.then_inc(gathered, 1)

            pe.wait_ge(mask_ready, 1)
            pe.matmul(bank[5][:, 0:EXPERTS], before[:, :], mask[:, 0, :], start=True, stop=True)
            pe.matmul(bank[5][:, EXPERTS:2 * EXPERTS], ones[:, :], mask[:, 0, :], start=True, stop=False)
            pe.wait_ge(b1_in, 32)
            pe.wait_ge(sel_ready, 1)
            bias(0, 0)
            pe.wait_ge(mask_ready, 2)
            pe.matmul(bank[5][:, EXPERTS:2 * EXPERTS], before[:, :], mask[:, 1, :], start=False, stop=True)
            pe.matmul(bank[5][:, 2 * EXPERTS:3 * EXPERTS], ones[:, :], mask[:, 0, :], start=True, stop=False)
            pe.matmul(bank[5][:, 2 * EXPERTS:3 * EXPERTS], ones[:, :], mask[:, 1, :], start=False, stop=True).then_inc(rank_mm, 1)
            bias(1, 0)

            def gate_up(pair, a, biased=False):
                e = pair * 2 + a
                if not biased:
                    pe.wait_ge(sel_ready, e + 1)
                    bias(0, a)
                    bias(1, a)
                for k in range(KT):
                    if a == 0 and k % (KT // 2) == 0:
                        pe.wait_ge(xT_ready, pair * 2 + (k // (KT // 2) + 1))
                    pe.wait_ge(w1_in[a][k], pair * 16 + 16)
                    for s, dst in enumerate((GATE, UP)):
                        for g in range(2):
                            at = s * FF + g * 512
                            last = pe.matmul(dst[g * CH:(g + 1) * CH, :], xT[:, k, a * CH:(a + 1) * CH], w1_of[a][:, k, at:at + 512], start=False, stop=True, skip_group_check=True)
                    last.then_inc(w1_used[a], 1)

            def expert_y(pair, a):
                e = pair * 2 + a
                pe.wait_ge(act_ready, e + 1)
                for q in range(4):
                    last = pe.transpose(ATP[:, q * P:(q + 1) * P], up_sb[:, q * P:(q + 1) * P], ident[:, :])
                last.then_inc(act_tr, 1)
                if a == 1:
                    pe.wait_ge(y_low, e)
                    pe.wait_ge(y_high, e)
                pe.matmul(YP[:, :], sel[a], b2_sb, start=True, stop=True)
                pe.wait_ge(actT_ready, e + 1)
                for k in range(KT):
                    pe.wait_ge(w2_in[k], e * 16 + 16)
                    g, q = divmod(k, 4)
                    for i in range(2):
                        last = pe.matmul(YP[i * CH:(i + 1) * CH, :], actT[:, q, g * CH:(g + 1) * CH], w2_sb[:, k, 512 * i:512 * i + 512], start=False, stop=True, skip_group_check=True)
                    last.then_inc(w2_used, 1)

            def two_experts(j, c, last):
                pair = j + PAIRS * c
                pe.wait_ge(up_ready, pair * 2 + 1)
                gate_up(pair, 1)
                if not last:
                    gather(pair + 2)
                pe.wait_ge(added, pair * 2 + 2)
                expert_y(pair, 0)
                if not last:
                    pe.wait_ge(up_ready, pair * 2 + 2)
                    gate_up(pair + 1, 0)
                pe.wait_ge(pickw_ready, pair + 1)
                for t in range(TT):
                    ins = pe.transpose(CTP[:, t * P:(t + 1) * P], pick_w[:, t, :], ident[:, :])
                ins.then_inc(pickw_tr, 1)
                expert_y(pair, 1)
                pe.wait_ge(comb_ready, pair + 1)
                pe.wait_ge(y_low, pair * 2 + 2)
                pe.wait_ge(y_high, pair * 2 + 2)
                for t, dsts in enumerate(((CMB, CTP), (ATP, YP))):
                    for i in range(2):
                        ins = pe.matmul(dsts[i][:, :], comb[:, t, :], y_sb[:, i, :], start=True, stop=True)
                    ins.then_inc(comb_mm, 1)

            def experts(c):
                pair = c * PAIRS
                if isinstance(c, int):
                    pe.wait_ge(h2_ready, TT)
                    gather(1)
                    pe.wait_ge(b2_in, 32)
                else:
                    pe.wait_ge(xT_ready, pair * 2)
                    gather(pair + 1)
                    pe.wait_ge(up_ready, pair * 2)
                gate_up(pair, 0, biased=isinstance(c, int))
                with pe.Fori(0, PAIRS - 1) as j:
                    two_experts(j, c, False)
                two_experts(PAIRS - 1, c, True)

            experts(0)
            pe.wait_ge(count_ready, 1)
            most = pe.value_load(cmax_i[0:1, 0:1], min_val=0, max_val=SEQ)
            with pe.If(most > CH):
                with pe.Fori(1, PASSES) as c:
                    with pe.If(most > c * CH):
                        experts(c)

        @block.vector
        def _(dve):
            n_step = [0]

            def link(ins):
                n_step[0] += 1
                ins.then_inc(dve_step, 1)
                dve.wait_ge(dve_step, n_step[0])

            def bc(ap, *shape):
                return ap.to_broadcast(list(shape))

            mult, add, sub = ALU.mult, ALU.add, ALU.subtract
            dve.wait_ge(pos_in, 16)
            dve.tensor_copy(pos_f[:, :], pos_i[:, :]).then_inc(pos_ready, 1)

            def scaled(col, width, size, last=True):
                i = dve.tensor_scalar(ms[:, col:col + width], ss[:, col:col + width], 1.0 / size, EPS, mult, add)
                if last:
                    i.then_inc(ms_ready, 1)

            for t in range(TT):
                dve.wait_ge(x_sq, t + 1)
                scaled(t, 1, D)
            dve.wait_ge(par_tr, 1)
            dve.tensor_copy(parT[:, 0:31], bank[7][:, 0:31])
            link(dve.tensor_copy(parT[:, 32:34], bank[7][:, 32:34]))
            for t in range(TT):
                dve.wait_ge(rs_ready, t + 1)
                dve.tensor_scalar(h_sb[:, t, :], x_sb[:, t, :], rs[:, t:t + 1], None, mult).then_inc(h_ready, 1)

            def norm_out(t, i, g, done):
                dve.tensor_tensor(hT[:, 4 * i:4 * i + 4, t * P:(t + 1) * P], bank[2 * t + i][:, :].rearrange("p (k s) -> p k s", s=P),
                                  bc(parT[:, g + 4 * i:g + 4 * i + 4].unsqueeze(2), P, 4, P), mult).then_inc(done, 1)

            for t in range(TT):
                for i in range(2):
                    dve.wait_ge(h_tr, 2 * t + i + 1)
                    norm_out(t, i, G1, hT_ready)

            dve.wait_ge(consts, 2)
            ang, kk, r, z, sp_, cp_, sn_, cs_ = rope_t
            for t in range(TT):
                last = dve.tensor_scalar(ang[:, t, :], invf[:, :], parT[:, 32 + t:33 + t], None, mult)
            link(last)
            two_pi = 2 * np.pi
            c1 = 6.28125
            c2 = float(np.round((two_pi - c1) * 2 ** 17) / 2 ** 17)
            c3 = two_pi - c1 - c2
            magic = 1.5 * 2 ** 23
            link(dve.tensor_scalar(kk, ang, 1 / two_pi, magic, mult, add))
            link(dve.tensor_scalar(kk, kk, -magic, None, add))
            link(dve.scalar_tensor_tensor(r, kk, -c1, ang, mult, add))
            link(dve.scalar_tensor_tensor(r, kk, -c2, r, mult, add))
            link(dve.scalar_tensor_tensor(r, kk, -c3, r, mult, add))
            link(dve.tensor_scalar(r, r, 0.5, None, mult))
            link(dve.tensor_tensor(z, r, r, mult))
            s_c, c_c, f = [], [], 1.0
            for i in range(1, 14):
                f *= i
                (s_c if i % 2 else c_c).append((-1) ** (i // 2) / f)
            s_c = s_c[1:]
            dve.tensor_scalar(sp_, z, s_c[-1], None, mult)
            link(dve.tensor_scalar(cp_, z, c_c[-1], None, mult))
            for i in range(len(s_c) - 2, -1, -1):
                dve.scalar_tensor_tensor(sp_, sp_, s_c[i], z, add, mult)
                link(dve.scalar_tensor_tensor(cp_, cp_, c_c[i], z, add, mult))
            dve.scalar_tensor_tensor(sn_, sp_, 1.0, r, add, mult)
            link(dve.tensor_scalar(cs_, cp_, 1.0, None, add))
            cos_t, sin_t = (v[:, :].rearrange("p (t r) -> p t r", t=TT) for v in (cos_sb, sin_sb))
            dve.scalar_tensor_tensor(sin_t, sn_, 2.0, cs_, mult, mult)
            link(dve.scalar_tensor_tensor(cos_t, sn_, -2.0, sn_, mult, mult))
            link(dve.tensor_scalar(cos_t, cos_t, 1.0, None, add))

            dve.wait_ge(gains_in, 32)
            for t in range(TT):
                raw = bank[4 + 2 * t]
                dve.wait_ge(lat_sq, t + 1)
                scaled(2 + 2 * t, 1, QL, last=False)
                scaled(3 + 2 * t, 1, KVL)
                dve.tensor_tensor(krg[:, t, :], raw[:, QL + KVL:A_COLS], kg_sb[:, NOPE:QK], mult)
                dve.wait_ge(rs_ready, 3 + t)
                dve.tensor_scalar(lat[:, t, 0:QL], raw[:, 0:QL], rs[:, 2 + 2 * t:3 + 2 * t], None, mult)
                dve.tensor_scalar(lat[:, t, QL:], raw[:, QL:QL + KVL], rs[:, 3 + 2 * t:4 + 2 * t], None, mult).then_inc(lat_ready, 1)
                dve.wait_ge(lat_tr, t + 1)
                dve.tensor_tensor(latT[:, :, t * P:(t + 1) * P], bank[5 + 2 * t][:, 0:3 * P].rearrange("p (k s) -> p k s", s=P),
                                  bc(parT[:, GL:GL + 3].unsqueeze(2), P, 3, P), mult).then_inc(latT_ready, 1)

            def rotate(src, tmp, dst, cos, sin, shape):
                t1, t2 = src(0), src(1)
                dve.tensor_tensor(tmp[0], t1, cos, mult)
                dve.tensor_tensor(tmp[1], t2, sin, mult)
                dve.tensor_tensor(tmp[2], t1, sin, mult)
                link(dve.tensor_tensor(tmp[3], t2, cos, mult))
                dve.tensor_tensor(dst(0), tmp[0], tmp[1], sub)
                return dve.tensor_tensor(dst(1), tmp[2], tmp[3], add)

            link(rotate(lambda i: krg[:, :, i * HR:(i + 1) * HR], krot_tmp,
                        lambda i: krot[:, :].rearrange("p (t r) -> p t r", t=TT)[:, :, i * HR:(i + 1) * HR],
                        cos_t, sin_t, None))
            for t in range(TT):
                dve.wait_ge(q_sq, t + 1)
                for i in range(2):
                    last = dve.tensor_tensor(q_sb[:, t, 4 * i:4 * i + 4, :], bank[2 * t + i][:, 0:4 * QK].rearrange("p (h d) -> p h d", d=QK),
                                             bc(qg_sb[:, :].unsqueeze(1), P, 4, QK), mult)
                last.then_inc(q_out, 1)
            for t in range(TT):
                dve.tensor_reduce(ss[:, 8 + 8 * t:16 + 8 * t], sq_q[t], AX.X, add)
            for t in range(TT):
                dve.wait_ge(v_out, t + 1)
                for i in range(2):
                    kv = bank[4 + 2 * t + i][:, :].rearrange("p (h d) -> p h d", d=NOPE + VH)
                    last = dve.tensor_tensor(kvx[:, t, 4 * i:4 * i + 4, 0:NOPE], kv[:, :, 0:NOPE],
                                             bc(kg_sb[:, 0:NOPE].unsqueeze(1), P, 4, NOPE), mult)
                last.then_inc(k_out, 1)
            for t in range(TT):
                last = dve.tensor_reduce(ss[:, 24 + 8 * t:32 + 8 * t], sq_k[t], AX.X, add)
            link(last)
            for t in range(TT):
                last = dve.tensor_scalar(ss[:, 24 + 8 * t:32 + 8 * t], ss[:, 24 + 8 * t:32 + 8 * t], ss[:, 6 + t:7 + t], None, add)
            link(last)
            scaled(8, 32, QK)
            wide = [bc(v.unsqueeze(2), P, TT, HEADS, HR) for v in (cos_t, sin_t)]
            half = lambda i: q_sb[:, :, :, NOPE + i * HR:NOPE + (i + 1) * HR]
            dve.wait_ge(q_out, 2)
            rotate(half, rot_tmp, half, wide[0], wide[1], None).then_inc(q_ready, 1)
            dve.wait_ge(rs_ready, 5)
            dve.wait_ge(k_out, 2)
            for t in range(TT):
                rk = rs[:, 24 + 8 * t:32 + 8 * t].unsqueeze(2)
                dve.tensor_tensor(kvx[:, t, :, 0:NOPE], kvx[:, t, :, 0:NOPE], bc(rk, P, HEADS, NOPE), mult)
                last = dve.tensor_tensor(kvx[:, t, :, NOPE:QK], bc(krot[:, t * ROPE:(t + 1) * ROPE].unsqueeze(1), P, HEADS, ROPE),
                                         bc(rk, P, HEADS, ROPE), mult)
            last.then_inc(k_ready, 1)
            link(dve.tensor_scalar(rq[:, :].rearrange("p (h t) -> p t h", t=TT), rs[:, 8:24].rearrange("p (t h) -> p t h", t=TT),
                                   float(QK) ** -0.5, None, mult))

            def conv(f):
                u, b = bank[2 * (f % 2)][:, 0:SEQ], bank[2 * (f % 2) + 1][:, 0:SEQ]
                c, y = cu[f % 2], y_tmp[f % 2]
                w = [parT[:, GC + CT * i + f:GC + CT * i + f + 1] for i in range(3)]
                if f < 2:
                    dve.memset(c[:, 0:1], 0.0)
                    dve.memset(c[:, SEQ + 1:SEQ + 2], 0.0)
                dve.wait_ge(c_out, f + 1)
                link(dve.tensor_tensor(c[:, 1:SEQ + 1], u, c_sb[f % 2], mult))
                link(dve.tensor_scalar(y, c[:, 0:SEQ], w[0], None, mult))
                link(dve.scalar_tensor_tensor(y, c[:, 1:SEQ + 1], w[1], y, mult, add))
                link(dve.scalar_tensor_tensor(y, c[:, 2:SEQ + 2], w[2], y, mult, add))
                dve.wait_ge(b_mm, f + 1)
                dve.tensor_tensor(yT[:, f, :], b, y, mult).then_inc(yT_ready, 1)

            def head_max(h):
                dve.wait_ge(s_mm, h + 1)
                pair = slice(TT * h, TT * h + TT)
                link(dve.tensor_reduce(mx[:, pair], bank[4 + h % 2][:, :].rearrange("p (t s) -> p t s", t=TT), AX.X, ALU.max))
                dve.scalar_tensor_tensor(nm[:, pair], mx[:, pair], -1.0, rq[:, pair], mult, mult).then_inc(max_ready, 1)

            def head_norm(h):
                dve.wait_ge(exp_ready, h + 1)
                pair = slice(TT * h, TT * h + TT)
                link(dve.reciprocal(rsum[:, pair], sums[:, pair]))
                for t in range(TT):
                    last = dve.tensor_scalar(prob[h % 2][:, t, :], prob[h % 2][:, t, :], rsum[:, TT * h + t:TT * h + t + 1], None, mult)
                last.then_inc(p_norm, 1)

            conv(0)
            for i in range(4):
                t, g = i // 2, i % 2
                dve.wait_ge(k_tr, i + 1)
                dve.tensor_copy(kT[0:QK, 4 * g:4 * g + 4, t * P:(t + 1) * P], bank[4 + i][0:QK, :].rearrange("p (h s) -> p h s", s=P)).then_inc(kT_ready, 1)
            head_max(0)
            head_norm(0)
            conv(1)
            for h in range(HEADS):
                if h + 1 < HEADS:
                    head_max(h + 1)
                    head_norm(h + 1)
                if h in (3, 6):
                    conv(2 if h == 3 else 3)

            for d in range(KT):
                dve.wait_ge(sig_ready, d + 1)
                dve.wait_ge(y_mm, d + 1)
                g = gated[d % 2]
                link(dve.tensor_tensor(g, sig[d % 2], bank[2 * (d % 2) + 1][:, :].rearrange("p (g s) -> p g s", s=SEQ), mult))
                dve.tensor_tensor(mergedT[:, d, :], g[:, 0, :], g[:, 1, :], add).then_inc(merged, 1)
            def x1_add(t, i):
                dve.wait_ge(x1_mm, 2 * t + i + 1)
                cols = slice(512 * i, 512 * i + 512)
                dve.tensor_tensor(x_sb[:, t, cols], bank[4 + 2 * t + i][:, :], x_sb[:, t, cols], add).then_inc(x1_ready, 1)

            def x1T_out(t, i):
                dve.wait_ge(x1_tr, 2 * t + i + 1)
                norm_out(t, i, G2, x1T_ready)

            def x1_norm(t):
                dve.wait_ge(x1_sq, t + 1)
                link(dve.tensor_tensor(ss[:, 40 + 2 * t:41 + 2 * t], ss[:, 40 + 2 * t:41 + 2 * t], ss[:, 41 + 2 * t:42 + 2 * t], add))
                dve.tensor_scalar(ms[:, 40 + t:41 + t], ss[:, 40 + 2 * t:41 + 2 * t], 1.0 / D, EPS, mult, add).then_inc(ms_ready, 1)

            def route(t):
                eight = slice(8 * t, 8 * t + 8)
                dve.wait_ge(rs_ready, 6 + t)
                dve.wait_ge(logit_mm, t + 1)
                link(dve.scalar_tensor_tensor(logit[:, t, :], bank[4 + 2 * t][:, 0:EXPERTS], rs[:, 40 + t:41 + t], rb_sb[:, :], mult, add))
                link(dve.max(top[:, eight], logit[:, t, :]))
                link(dve.max_index(topi[:, eight], top[:, eight], logit[:, t, :]))
                link(dve.tensor_tensor(first4, expert_no[:, :].rearrange("p (j e) -> p j e", j=TOPK),
                                       bc(topi[:, 8 * t:8 * t + TOPK].unsqueeze(2), P, TOPK, EXPERTS), ALU.is_equal))
                dve.tensor_reduce(mask[:, t, :], first4.rearrange("p j e -> p e j"), AX.X, add).then_inc(mask_ready, 1)
                dve.tensor_scalar(ntop[:, t:t + 1], top[:, 8 * t:8 * t + 1], -1.0, None, mult).then_inc(ntop_ready, 1)

            def first_selectors():
                for a in range(2):
                    dve.tensor_scalar(sel[a], half_mask, one_hot[:, a:a + 1], None, mult).then_inc(sel_ready, 1)

            dve.wait_ge(consts2, 1)
            first_selectors()
            dve.wait_ge(rb_in, 16)
            x1_add(0, 0)
            x1_add(0, 1)
            x1_norm(0)
            x1_add(1, 0)
            x1T_out(0, 0)
            x1T_out(0, 1)
            x1T_out(1, 0)
            route(0)
            x1_add(1, 1)
            x1T_out(1, 1)
            x1_norm(1)
            route(1)
            dve.wait_ge(mask_ready, 2)
            dve.wait_ge(rank_mm, 1)
            link(dve.scalar_tensor_tensor(rank[:, :, 0:EXPERTS], bank[5][:, 0:2 * EXPERTS].rearrange("p (t e) -> p t e", t=TT), 1.0, mask, add, mult))

            def build_pick(cols):
                for t in range(TT):
                    for a in range(2):
                        last = dve.tensor_scalar(pick[:, t, a * CH:(a + 1) * CH], slots[:, :], rank[:, t, cols[a]], None, ALU.is_equal)
                last.then_inc(pick_ready, 1)

            def gather_out(count):
                for i, src in enumerate((XTP0, XTP1)):
                    dve.wait_ge(gathered, count * 2 + (i - 1))
                    dve.tensor_tensor(xT[:, 4 * i:4 * i + 4, :], src[:, :].rearrange("p (k s) -> p k s", s=P),
                                      bc(parT[:, G2 + 4 * i:G2 + 4 * i + 4].unsqueeze(2), P, 4, P), mult).then_inc(xT_ready, 1)

            def swiglu(pair, a, first=False):
                e = pair * 2 + a
                dve.wait_ge(w1_used[a], pair * KT + 2 * KT)
                dve.tensor_scalar(gate_sb, GATE[:, :], LIMIT, None, ALU.min).then_inc(gate_ready, 1)
                if not first:
                    dve.wait_ge(act_tr, e)
                dve.tensor_scalar(up_sb, UP[:, :], LIMIT, -LIMIT, ALU.min, ALU.max).then_inc(up_ready, 1)
                dve.wait_ge(up_ready, e + 1)
                dve.scalar_tensor_tensor(up_sb, up_sb, 1.0, gate_sb, add, mult).then_inc(prod_ready, 1)
                dve.wait_ge(prod_ready, e + 1)
                dve.wait_ge(esig_ready, e + 1)
                dve.tensor_tensor(up_sb, up_sb, sg_sb, mult).then_inc(act_ready, 1)

            def output_half(pair, a, next_col):
                used = pair * (2 * KT) + (a * KT + KT)
                if next_col is not None:
                    dve.wait_ge(w2_used, used + 1)
                    dve.tensor_scalar(sel[a], half_mask, one_hot[:, next_col], None, mult).then_inc(sel_ready, 1)
                dve.wait_ge(w2_used, used + KT)
                dve.tensor_copy(y_sb[a * CH:(a + 1) * CH, 0, :], YP[0:CH, :]).then_inc(y_low, 1)

            def two_experts(j, c, last):
                pair = j + PAIRS * c
                if not last:
                    build_pick([ds(j * 2 + 2, 1), ds(j * 2 + 3, 1)])
                for t in range(TT):
                    for a in range(2):
                        ins = dve.tensor_scalar(pick_w[:, t, a * CH:(a + 1) * CH], slots[:, :], rank[:, t, ds(j * 2 + a, 1)], wd[:, t, ds(j * 2 + a, 1)], ALU.is_equal, mult)
                ins.then_inc(pickw_ready, 1)
                swiglu(pair, 1)
                if not last:
                    gather_out(pair + 2)
                output_half(pair, 0, None if last else ds(j * 2 + 2, 1))
                if not last:
                    swiglu(pair + 1, 0)
                output_half(pair, 1, None if last else ds(j * 2 + 3, 1))
                for t, dsts in enumerate(((CMB, CTP), (ATP, YP))):
                    dve.wait_ge(comb_mm, pair * 2 + (t + 1))
                    for i in range(2):
                        cols = slice(512 * i, 512 * i + 512)
                        ins = dve.tensor_tensor(x_sb[:, t, cols], dsts[i][:, :], x_sb[:, t, cols], add)
                    ins.then_inc(added, 1)

            def experts(c):
                if not isinstance(c, int):
                    dve.tensor_scalar(rank[:, :, :], rank[:, :, :], -float(CH), None, add).then_inc(rank_moved, 1)
                    dve.wait_ge(rank_moved, c)
                build_pick([slice(0, 1), slice(1, 2)])
                if not isinstance(c, int):
                    first_selectors()
                if isinstance(c, int):
                    link(dve.tensor_reduce(cmax[:, :], bank[5][:, 2 * EXPERTS:3 * EXPERTS], AX.X, ALU.max))
                    dve.tensor_copy(cmax_i[:, :], cmax[:, :]).then_inc(count_ready, 1)
                gather_out(c * PAIRS + 1)
                if isinstance(c, int):
                    for t in range(TT):
                        dve.wait_ge(ew_ready, t + 1)
                        last = dve.scalar_tensor_tensor(ew[:, t, :], ew[:, t, :], 1.0, mask[:, t, :], mult, mult, accum_out=esum[:, t:t + 1])
                    link(last)
                    link(dve.reciprocal(ersum[:, :], esum[:, :]))
                    for t in range(TT):
                        last = dve.tensor_scalar(wd[:, t, :], ew[:, t, :], ersum[:, t:t + 1], None, mult)
                    last.then_inc(added, TT)
                    dve.wait_ge(added, TT)
                swiglu(c * PAIRS, 0, first=isinstance(c, int))
                with dve.Fori(0, PAIRS - 1) as j:
                    two_experts(j, c, False)
                two_experts(PAIRS - 1, c, True)

            experts(0)
            dve.wait_ge(count_ready, 1)
            most = dve.value_load(cmax_i[0:1, 0:1], min_val=0, max_val=SEQ)
            with dve.If(most > CH):
                with dve.Fori(1, PASSES) as c:
                    with dve.If(most > c * CH):
                        experts(c)


_INS = ['x', 'positions', 'norm1_g', 'w_in', 'q_a_norm_g', 'kv_a_norm_g', 'w_uq', 'w_ukv', 'q_norm_g', 'k_norm_g',
        'conv_w', 'w_o_mla', 'w_o_conv', 'w_o', 'norm2_g', 'router_w', 'router_b', 'expert_w1', 'expert_b1',
        'expert_w2', 'expert_b2']


def kernel(**inputs):
    import numpy as _np
    import concourse.bacc as _bacc
    from concourse import mybir as _mybir
    from concourse.bass_utils import run_bass_kernel_spmd as _run

    nc = _bacc.Bacc("TRN2", target_bir_lowering=False, num_devices=1)
    arrays, args = {}, []
    for name in _INS:
        a = _np.ascontiguousarray(inputs[name])
        arrays[f"in_{name}"] = a
        args.append(nc.dram_tensor(f"in_{name}", a.shape, _mybir.dt.from_np(a.dtype), kind="ExternalInput").ap())
    args.append(nc.dram_tensor("out_x", (1, SEQ, D), _mybir.dt.float32, kind="ExternalOutput").ap())
    build(nc, *args)
    r = _run(nc, [arrays], core_ids=[0])
    return r.results[0]["out_x"]
```

```python
import concourse.bass as bass
from concourse import mybir
from contextlib import ExitStack
import numpy as np

D, SEQ, P = 1024, 256, 128
TT, KT = SEQ // P, D // P
HEADS, NOPE, ROPE, VH = 8, 64, 32, 64
QK = NOPE + ROPE
HR = ROPE // 2
QL, KVL, CW = 256, 128, 512
A_COLS = QL + KVL + ROPE
CT = CW // P
EXPERTS, TOPK, FF = 32, 4, 1024
CH = 64
PASSES = SEQ // CH
WHOLE = 4
PAIRS = EXPERTS // 2
KVX = NOPE + ROPE + VH
SMALL = 2793
WARM = 10
EPS = 1e-6
THETA = 10000.0
LIMIT, ALPHA = 7.0, 1.702


def build(nc, x, positions, norm1_g, w_in, q_a_norm_g, kv_a_norm_g, w_uq, w_ukv, q_norm_g, k_norm_g,
          conv_w, w_o_mla, w_o_conv, w_o, norm2_g, router_w, router_b, expert_w1, expert_b1,
          expert_w2, expert_b2, out):
    fp32, i32, u32 = mybir.dt.float32, mybir.dt.int32, mybir.dt.uint32
    part32 = mybir.dt.float32r
    ALU, ACT, AX = mybir.AluOpType, mybir.ActivationFunctionType, mybir.AxisListType
    ds = bass.ds

    ctx = ExitStack()
    with ctx:
        def sb(name, cols, dt=fp32, rows=P):
            return ctx.enter_context(nc.sbuf_tensor(name, [rows, cols], dt))

        def sem(name):
            return ctx.enter_context(nc.semaphore(name))

        def view(region, at, *shape, rows=P):
            n = int(np.prod(shape))
            part = region[0:rows, at:at + n]
            if len(shape) == 1:
                return part
            names = "abc"[:len(shape)]
            text = f"p ({' '.join(names)}) -> p {' '.join(names)}"
            return part.rearrange(text, **{c: s for c, s in zip(names[1:], shape[1:])})

        def regions(stack, kind):
            return [stack.enter_context(nc.sbuf_tensor(name + kind, [P, cols], fp32)) for name, cols in (
                ("W1", KT * 2 * FF),
                ("W2", KT * D),
                ("W1B", KT * 2 * FF + SMALL),
                ("HT", KT * SEQ),
                ("OT", 1024),
                ("YB", 1024))]

        with ExitStack() as names:
            W1, W2, W1B, HT, OT, YB = regions(names, "")
        W1_PARTS, W2_PARTS, W1B_PARTS, HT_PARTS, OT_PARTS, YB_PARTS = regions(ctx, "_parts")
        X = sb("X", TT * D)
        H = sb("H", TT * D)
        WA, ATT = W1B[:, 0:9984], W1B[:, 9984:9984 + 9024]
        SM = W1B[:, KT * 2 * FF:]

        w1_sb = view(W1, 0, KT, 2 * FF)
        w2_sb = view(W2, 0, KT, D)
        w_gates = [view(W1, i * 4096, KT, 2, 2 * P) for i in range(KT // 2)]
        w_o_sb = [view(W1, i * 4096, KT, 512) for i in range(2)]
        w_uc = w2_sb
        w_mla = view(W2, 0, CT, D)
        w_cnv = view(W2, CT * D, CT, D)
        w_branch = view(W2, 0, 2 * CT, D)
        w_a = view(WA, 0, KT, A_COLS)
        w_uq_sb = view(WA, 3328, 2, HEADS * QK)
        w_ukv_sb = WA[:, 4864:5888]
        w_b = view(WA, 5888, KT, CW)
        cu = [view(WA, i * 258, 258) for i in range(2)]
        c_sb = [view(WA, 520 + i * 256, 256) for i in range(2)]
        y_tmp = [view(WA, 1032 + i * 256, 256) for i in range(2)]
        krot = WA[:, 2832:2832 + TT * ROPE]
        mx, nm, sums, rsum = (WA[:, 2896 + i * 16:2912 + i * 16] for i in range(4))
        rot_tmp = [view(WA, 1600 + i * 256, TT, HEADS, HR) for i in range(4)]
        krot_tmp = [view(WA, 2640 + i * 32, TT, HR) for i in range(4)]

        x_sb = view(X, 0, TT, D)
        h_sb = view(H, 0, TT, D)
        sq_a = [H[:, 1536:1536 + A_COLS], YB[:, 512:512 + A_COLS]]
        sq_q = [view(H, 768 * t, HEADS, QK) for t in range(TT)]
        sq_k = [view(YB, 512 * t, HEADS, NOPE) for t in range(TT)]
        prob = [view(H, 512 * i, TT, SEQ) for i in range(2)]
        prob_t = [view(H, 1024 + 512 * i, TT, SEQ) for i in range(2)]
        sig = [view(H, 512 * i, 2, SEQ) for i in range(2)]
        gated = [view(H, 1024 + 512 * i, 2, SEQ) for i in range(2)]
        hT = view(HT, 0, KT, SEQ)

        q_sb = view(ATT, 0, TT, HEADS, QK)
        kvx = view(ATT, 1536, TT, HEADS, KVX)
        qT = view(ATT, 4096, HEADS, SEQ)
        kT = view(ATT, 6144, HEADS, SEQ)
        lat = view(ATT, 8192, TT, QL + KVL)
        krg = view(ATT, 8960, TT, ROPE)
        latT = view(OT, 0, 3, SEQ)
        oT = view(OT, 0, CT, SEQ)
        yT = view(YB, 0, CT, SEQ)
        rope_t = [view(YB, 32 * i, TT, HR) for i in range(8)]

        w_uc_low, w_b_low = view(W2_PARTS, 0, KT, D), view(W1B_PARTS, 5888, KT, CW)
        hT_early = [view(W1_PARTS, 8192 + i * KT * SEQ, KT, SEQ) for i in range(2)]
        conv_up = [view(W1_PARTS, 12288 + i * D, KT, P) for i in range(3)]
        gates_up_early = [view(W1_PARTS, 12288 + i * 2 * FF, KT, 2, P) for i in range(2)]
        hT_parts = (view(W1B_PARTS, 3 * 2 * FF, KT, SEQ), view(HT_PARTS, 0, KT, SEQ))
        ocT_up = view(W1B_PARTS, KT * 2 * FF, 2 * CT, SEQ)
        ocT_low = (view(OT_PARTS, 0, CT, SEQ), view(YB_PARTS, 0, CT, SEQ))
        gates_up = [view(W1B_PARTS, (4 + i) * 2 * FF, KT, 2, P) for i in range(2)]
        gates_low = [view(W1_PARTS, i * 4096, KT, 2, 2 * P) for i in range(KT // 2)]
        branch_up = [view(W1B_PARTS, 6 * 2 * FF + i * FF, 2 * CT, P) for i in range(2)]
        branch_low = view(W2_PARTS, 0, 2 * CT, D)
        mergedT = view(W1B, (KT - 1) * 2 * FF, KT, SEQ)
        w1b_sb = view(W1B, 0, KT, 2 * FF)
        w1_of = (w1b_sb, w1_sb)
        xT = view(HT, 0, KT, P)
        gate_sb, up_sb = HT[:, 1024:1536], HT[:, 1536:2048]
        sg_sb = YB[:, 0:512]
        comb = view(YB, 512, TT, P)
        pick_w = view(YB, 768, TT, P)
        y_sb = view(OT, 0, 2, 512)
        b1_sb = view(SM, 0, 2, 512, rows=2 * EXPERTS)
        b2_sb = SM[0:2 * EXPERTS, 1024:1536]
        rw_sb = view(SM, 1536, KT, EXPERTS)
        actT = view(SM, 1536, 4, P)
        pick = view(SM, 2048, TT, P)
        sel = [SM[0:2 * EXPERTS, 2304 + P * i:2304 + P * (i + 1)] for i in range(2)]
        half_mask = SM[0:2 * EXPERTS, 2560:2688]
        rank = view(SM, 2688, TT, EXPERTS + 2)
        one_hot = SM[0:2 * EXPERTS, 2756:2756 + EXPERTS + 2]
        logit = view(OT, 0, TT, EXPERTS)
        mask = view(OT, 64, TT, EXPERTS)
        ew = view(OT, 128, TT, EXPERTS)
        first4 = view(OT, 192, TOPK, EXPERTS)
        top = OT[:, 320:336]
        topi = OT[:, 336:352].bitcast(u32)
        ntop, esum, ersum = (OT[:, 352 + TT * i:354 + TT * i] for i in range(3))
        wd_sb = sb("wd", TT * EXPERTS)
        ident = sb("ident", P)
        wd = wd_sb[:, :].rearrange("p (t e) -> p t e", t=TT)
        before = sb("before", P)
        ones = sb("ones", P)
        slots = sb("slots", CH)
        expert_no = sb("expert_no", TOPK * EXPERTS)
        qg_sb, kg_sb = sb("qg_sb", QK), sb("kg_sb", QK)
        rb_sb = sb("rb_sb", EXPERTS)
        par = ATT[0:32, 0:P]
        pos_i = ATT[0:TT, P:2 * P].bitcast(i32)
        pos_f = ATT[0:TT, 2 * P:3 * P]
        parT = sb("parT", 34)
        invf = sb("invf", HR)
        mhalf = sb("mhalf", 32)
        cos_sb, sin_sb = sb("cos_sb", TT * HR), sb("sin_sb", TT * HR)
        ss, ms, rs = sb("ss", 48), sb("ms", 48), sb("rs", 48)
        rq = sb("rq", 16)
        cmax = sb("cmax", 1)
        cmax_i = sb("cmax_i", 1, i32)

        G1, G2, GL, GC = 0, 8, 16, 19

        bank = [ctx.enter_context(nc.psum_tensor(f"bank{i}", [P, 512], fp32)) for i in range(8)]
        GATE, UP, XTP0, XTP1, CTP, ATP, YP, CMB = bank

        def gates_up_of(d):
            return (gates_up_early if d < 2 else gates_up)[d % 2]

        x_in = [sem(f"x_in{t}") for t in range(TT)]
        par_in, pos_in, gains_in, rb_in = sem("par_in"), sem("pos_in"), sem("gains_in"), sem("rb_in")
        wa_in = [sem(f"wa_in{i}") for i in range(2)]
        uq_in, ukv_in, b_in = sem("uq_in"), sem("ukv_in"), sem("b_in")
        uc_in = [sem(f"uc_in{i}") for i in range(2)]
        gates_in = [sem(f"gates_in{i}") for i in range(4)]
        mla_in, cnv_in = sem("mla_in"), sem("cnv_in")
        wo_in = [sem(f"wo_in{i}") for i in range(2)]
        router_in, b1_in, b2_in = sem("router_in"), sem("b1_in"), sem("b2_in")
        w1_in = [[sem(f"w1{'ab'[a]}_in{k}") for k in range(KT)] for a in range(2)]
        w2_in = [sem(f"w2_in{k}") for k in range(KT)]
        stored = [sem(f"stored{n}") for n in range(2 * TT)]
        consts, consts2 = sem("consts"), sem("consts2")
        pool_step, dve_step = sem("pool_step"), sem("dve_step")
        pos_ready, par_tr, x_sq, ms_ready, rs_ready = (sem(n) for n in ("pos_ready", "par_tr", "x_sq", "ms_ready", "rs_ready"))
        h_ready, h_tr, hT_ready = sem("h_ready"), sem("h_tr"), sem("hT_ready")
        lat_mm, lat_sq, lat_ready, lat_tr, latT_ready = (sem(n) for n in ("lat_mm", "lat_sq", "lat_ready", "lat_tr", "latT_ready"))
        q_mm, kv_mm, q_sq, q_out, k_out, v_out = (sem(n) for n in ("q_mm", "kv_mm", "q_sq", "q_out", "k_out", "v_out"))
        q_ready, k_ready, q_tr, k_tr, qT_ready, kT_ready = (sem(n) for n in ("q_ready", "k_ready", "q_tr", "k_tr", "qT_ready", "kT_ready"))
        uc_mm, b_mm, c_out, yT_ready = sem("uc_mm"), sem("b_mm"), sem("c_out"), sem("yT_ready")
        s_mm, max_ready, exp_ready, p_norm, p_tr, pT_ready, o_mm, oT_ready = (
            sem(n) for n in ("s_mm", "max_ready", "exp_ready", "p_norm", "p_tr", "pT_ready", "o_mm", "oT_ready"))
        hT_up_ready, hT_low_ready, ocT_up_ready, ocT_low_ready = (
            sem(n) for n in ("hT_up_ready", "hT_low_ready", "ocT_up_ready", "ocT_low_ready"))
        conv_up_w, conv_low_w = sem("conv_up_w"), sem("conv_low_w")
        gate_up_w, gate_low_w, branch_up_w, branch_low_w = (
            sem(n) for n in ("gate_up_w", "gate_low_w", "branch_up_w", "branch_low_w"))
        gate_mm, y_mm, sig_ready, merged = sem("gate_mm"), sem("y_mm"), sem("sig_ready"), sem("merged")
        x1_mm, x1_ready, x1_sq, h2_ready, x1_tr, x1T_ready = (
            sem(n) for n in ("x1_mm", "x1_ready", "x1_sq", "h2_ready", "x1_tr", "x1T_ready"))
        logit_mm, ntop_ready, ew_ready, mask_ready, rank_mm, count_ready = (
            sem(n) for n in ("logit_mm", "ntop_ready", "ew_ready", "mask_ready", "rank_mm", "count_ready"))
        pick0_ready = sem("pick0_ready")
        pick_ready, sel_ready, pickw_ready = sem("pick_ready"), sem("sel_ready"), sem("pickw_ready")
        gathered, xT_ready, w2_used = (sem(n) for n in ("gathered", "xT_ready", "w2_used"))
        w1_used = [sem("w1a_used"), sem("w1b_used")]
        gate_ready, up_ready, esig_ready, prod_ready, act_ready = (
            sem(n) for n in ("gate_ready", "up_ready", "esig_ready", "prod_ready", "act_ready"))
        pass_stored, rank_moved, pickw_tr, comb_ready, act_tr, actT_ready, y_low, y_high, comb_mm, added = (
            sem(n) for n in ("pass_stored", "rank_moved", "pickw_tr", "comb_ready", "act_tr", "actT_ready", "y_low", "y_high", "comb_mm", "added"))

        block = ctx.enter_context(nc.Block())

        def rows(w):
            return w.rearrange("(k p) n -> p k n", p=P)

        @block.sync
        def _(sp):
            for t in range(TT):
                sp.dma_start(x_sb[:, t, :], x[0, t * P:(t + 1) * P, :]).then_inc(x_in[t], 16)
            sp.dma_start(pos_i[:, :], positions[0].rearrange("(t p) -> t p", p=P)).then_inc(pos_in, 16)
            sp.dma_start(par[G1:G1 + 8, :], norm1_g[0].rearrange("(k p) -> k p", p=P)).then_inc(par_in, 16)
            sp.dma_start(par[G2:G2 + 8, :], norm2_g[0].rearrange("(k p) -> k p", p=P)).then_inc(par_in, 16)
            sp.dma_start(par[GL:GL + 2, :], q_a_norm_g[0].rearrange("(k p) -> k p", p=P)).then_inc(par_in, 16)
            sp.dma_start(par[GL + 2:GL + 3, :], kv_a_norm_g[0].rearrange("(k p) -> k p", p=P)).then_inc(par_in, 16)
            sp.dma_start(par[GC:GC + 12, :], conv_w[0].rearrange("w (k p) -> (w k) p", p=P)).then_inc(par_in, 16)
            wi = rows(w_in[0])
            for i in range(2):
                sp.dma_start(w_a[:, 4 * i:4 * i + 4, :], wi[:, 4 * i:4 * i + 4, 0:A_COLS]).then_inc(wa_in[i], 16)
            sp.dma_start(w_uq_sb, rows(w_uq[0])).then_inc(uq_in, 16)
            sp.dma_start(w_ukv_sb, w_ukv[0]).then_inc(ukv_in, 16)
            for i in range(2):
                sp.dma_start(w_uc[:, 4 * i:4 * i + 4, :],
                             wi[:, 4 * i:4 * i + 4, A_COLS:A_COLS + 2 * CW]).then_inc(uc_in[i], 16)
            sp.dma_start(w_b, wi[:, :, A_COLS + 2 * CW:A_COLS + 3 * CW]).then_inc(b_in, 16)

            def load_gates(i):
                for g in range(2):
                    at = A_COLS + 3 * CW + g * D + i * 2 * P
                    sp.dma_start(w_gates[i][:, :, g, :], wi[:, :, at:at + 2 * P]).then_inc(gates_in[i], 16)

            load_gates(0)
            load_gates(1)
            sp.wait_ge(uc_mm, CT)
            sp.dma_start(w_mla, rows(w_o_mla[0])).then_inc(mla_in, 16)
            sp.dma_start(w_cnv, rows(w_o_conv[0])).then_inc(cnv_in, 16)
            sp.wait_ge(gate_mm, 2)
            load_gates(2)
            load_gates(3)
            sp.wait_ge(yT_ready, CT)
            sp.wait_ge(o_mm, HEADS)

            def load_experts(c):
                def load_w1(j, a, tiles=range(KT), free=False):
                    for k in tiles:
                        if not free:
                            sp.wait_ge(w1_used[a], (j + PAIRS * c) * KT + (k + 1))
                        sp.dma_start(w1_of[a][:, k, :], expert_w1[0, ds(j * 2 + a, 1), k * P:(k + 1) * P, :].rearrange("a p n -> p (a n)")).then_inc(w1_in[a][k], 16)

                def load_w2(j, a):
                    for k in range(KT):
                        sp.wait_ge(w2_used, (j + PAIRS * c) * (2 * KT) + (a * KT + k + 1))
                        sp.dma_start(w2_sb[:, k, :], expert_w2[0, ds(j * 2 + a, 1), k * P:(k + 1) * P, :].rearrange("a p n -> p (a n)")).then_inc(w2_in[k], 16)

                if isinstance(c, int):
                    load_w1(0, 0, range(3), free=True)
                    sp.wait_ge(gate_mm, KT // 2)
                    for i in range(2):
                        sp.dma_start(w_o_sb[i], rows(w_o[0])[:, :, 512 * i:512 * i + 512]).then_inc(wo_in[i], 16)
                    sp.wait_ge(gate_mm, 3 * KT // 4)
                    load_w1(0, 1, range(KT // 2, 3 * KT // 4), free=True)
                    sp.wait_ge(w1_used[1], KT // 2)
                    load_w1(0, 1, range(3 * KT // 4, KT), free=True)
                    sp.wait_ge(y_mm, KT)
                    sp.dma_start(rw_sb, rows(router_w[0])).then_inc(router_in, 16)
                    for i in range(2):
                        sp.dma_start(b1_sb[i * EXPERTS:(i + 1) * EXPERTS, :, :],
                                     expert_b1[0].rearrange("e (s h n) -> e s h n", s=2, h=2)[:, :, i, :]).then_inc(b1_in, 16)
                        sp.dma_start(b2_sb[i * EXPERTS:(i + 1) * EXPERTS, :],
                                     expert_b2[0].rearrange("e (h n) -> e h n", h=2)[:, i, :]).then_inc(b2_in, 16)
                    load_w1(0, 0, range(3, KT - 1), free=True)
                    load_w2(0, 0)
                    sp.wait_ge(w1_used[1], 3 * KT // 4)
                    load_w1(0, 1, range(KT // 4), free=True)
                    sp.wait_ge(w1_used[0], KT)
                    load_w1(0, 0, [KT - 1], free=True)
                    sp.wait_ge(w1_used[1], KT)
                    load_w1(0, 1, range(KT // 4, KT // 2), free=True)
                else:
                    load_w1(0, 0)
                    load_w2(0, 0)
                    load_w1(0, 1)
                load_w1(1, 0)
                load_w1(1, 1)
                load_w2(0, 1)
                load_w1(2, 0)
                load_w2(1, 0)
                load_w1(2, 1)
                load_w2(1, 1)
                load_w2(2, 0)
                with sp.Fori(2, PAIRS - 1) as j:
                    load_w1(j + 1, 0)
                    load_w2(j, 1)
                    load_w1(j + 1, 1)
                    load_w2(j + 1, 0)
                load_w2(PAIRS - 1, 1)

            load_experts(0)
            sp.wait_ge(count_ready, 1)
            most = sp.value_load(cmax_i[0:1, 0:1], min_val=0, max_val=SEQ)
            with sp.If(most > CH):
                with sp.Fori(1, PASSES) as c:
                    with sp.If(most > c * CH):
                        load_experts(c)
                        sp.wait_ge(added, c * (4 * PAIRS) + (4 * PAIRS + 4))
                        sp.sem_inc(pass_stored, 1)
            for n in range(2 * TT):
                sp.wait_ge(added, 4 * PAIRS + 1 + n)
                t, cols = n // 2, slice(512 * (n % 2), 512 * (n % 2) + 512)
                sp.dma_start(out[0, t * P:(t + 1) * P, cols], x_sb[:, t, cols]).then_inc(stored[n], 16)
            for n in range(2 * TT):
                sp.wait_ge(stored[n], 16)

        @block.gpsimd
        def _(pool):
            n = [0]

            def link(ins):
                n[0] += 1
                ins.then_inc(pool_step, 1)
                pool.wait_ge(pool_step, n[0])

            pool.memset(ident[:, :], 0.0)
            link(pool.memset(before[:, :], 1.0))
            pool.affine_select(out=ident[:, :], in_=ident[:, :], compare_op=ALU.not_equal, fill=1.0,
                               base=0, pattern=[[-1, P]], channel_multiplier=1).then_inc(consts, 1)
            pool.memset(mhalf[:, :], -0.5)
            inv = np.float32(THETA) ** (-np.arange(0, ROPE, 2, dtype=np.float32) / np.float32(ROPE))
            for i in range(HR):
                last = pool.memset(invf[:, i:i + 1], float(inv[i]))
            link(last)
            pool.affine_select(out=before[:, :], in_=before[:, :], compare_op=ALU.is_gt, fill=0.0,
                               base=0, pattern=[[1, P]], channel_multiplier=-1)
            pool.memset(ones[:, :], 1.0)
            pool.iota(slots[:, :], pattern=[[1, CH]], base=1, channel_multiplier=0,
                      allow_small_or_imprecise_dtypes=True)
            pool.iota(expert_no[:, :], pattern=[[0, TOPK], [1, EXPERTS]], base=0, channel_multiplier=0,
                      allow_small_or_imprecise_dtypes=True).then_inc(consts, 1)
            pool.dma_start(qg_sb[:, :], q_norm_g[0].partition_broadcast(P)).then_inc(gains_in, 16)
            pool.dma_start(kg_sb[:, :], k_norm_g[0].partition_broadcast(P)).then_inc(gains_in, 16)
            pool.dma_start(rb_sb[:, :], router_b[0].partition_broadcast(P)).then_inc(rb_in, 16)

            def power(at, width, k):
                pool.wait_ge(ms_ready, k)
                pool.tensor_tensor(rs[:, at:at + width], ms[:, at:at + width], mhalf[:, 0:width],
                                   ALU.pow).then_inc(rs_ready, 1)

            for t in range(TT):
                power(t, 1, 1 + t)
            for t in range(TT):
                power(2 + 2 * t, 2, 3 + t)
            power(8, 32, 5)
            pool.wait_ge(o_mm, HEADS)
            link(pool.memset(rank[:, :, EXPERTS:], -1.0))
            for i in range(2):
                rows_i = slice(i * EXPERTS, (i + 1) * EXPERTS)
                link(pool.memset(half_mask[rows_i, i * CH:(i + 1) * CH], 1.0))
                link(pool.memset(half_mask[rows_i, (1 - i) * CH:(2 - i) * CH], 0.0))
            link(pool.memset(one_hot, 0.0))
            for i in range(2):
                part = one_hot[i * EXPERTS:(i + 1) * EXPERTS, :]
                link(pool.affine_select(out=part, in_=part, compare_op=ALU.not_equal, fill=1.0,
                                        base=0, pattern=[[-1, EXPERTS + 2]], channel_multiplier=1))
            pool.sem_inc(consts2, 1)
            for t in range(TT):
                power(40 + t, 1, 6 + t)

        @block.scalar
        def _(act):
            def upper(dst, src):
                return act.activation(dst.bitcast(part32), src, ACT.Copy)

            def conv_upper(i):
                f, part = divmod(i, 3)
                act.wait_ge(b_in if part == 2 else uc_in[1], 16)
                if i < WHOLE + 3:
                    act.wait_ge(uc_in[0], 16)
                else:
                    act.wait_ge(b_mm if part == 2 else uc_mm, f)
                w = w_b[:, :, f * P:(f + 1) * P] if part == 2 else w_uc[:, :, part * CW + f * P:part * CW + (f + 1) * P]
                upper(conv_up[i % 3], w).then_inc(conv_up_w, 1)

            def gates_upper(d):
                act.wait_ge(gates_in[d // 2], 32)
                if d < 2:
                    act.wait_ge(b_mm if d else uc_mm, CT)
                if d >= 4:
                    act.wait_ge(gate_mm, d - 1)
                upper(gates_up_of(d), w_gates[d // 2][:, :, :, (d % 2) * P:(d % 2 + 1) * P]).then_inc(gate_up_w, 1)

            for t in range(TT):
                act.wait_ge(x_in[t], 16)
                act.activation(HT[:, t * D:(t + 1) * D], x_sb[:, t, :], ACT.Square,
                               accum_out=ss[:, t:t + 1]).then_inc(x_sq, 1)
            act.wait_ge(hT_ready, 2 * TT)
            upper(hT_early[0], hT).then_inc(hT_up_ready, 1)
            for t in range(TT):
                act.wait_ge(lat_mm, t + 1)
                for a, b, col in ((0, QL, 2 + 2 * t), (QL, QL + KVL, 3 + 2 * t), (QL + KVL, A_COLS, 6 + t)):
                    last = act.activation(sq_a[t][:, a:b], bank[4 + 2 * t][:, a:b], ACT.Square, accum_out=ss[:, col:col + 1])
                last.then_inc(lat_sq, 1)
            for t in range(TT):
                act.wait_ge(q_mm, t + 1)
                for i in range(2):
                    last = act.activation(sq_q[t][:, 4 * i:4 * i + 4, :],
                                          bank[2 * t + i][:, 0:4 * QK].rearrange("p (h d) -> p h d", d=QK), ACT.Square)
                last.then_inc(q_sq, 1)
            for t in range(TT):
                act.wait_ge(kv_mm, t + 1)
                for i in range(2):
                    kv = bank[4 + 2 * t + i][:, :].rearrange("p (h d) -> p h d", d=NOPE + VH)
                    act.activation(sq_k[t][:, 4 * i:4 * i + 4, :], kv[:, :, 0:NOPE], ACT.Square)
                for i in range(2):
                    kv = bank[4 + 2 * t + i][:, :].rearrange("p (h d) -> p h d", d=NOPE + VH)
                    last = act.activation(kvx[:, t, 4 * i:4 * i + 4, QK:KVX], kv[:, :, NOPE:], ACT.Copy)
                last.then_inc(v_out, 1)

            def conv_c(f):
                act.wait_ge(uc_mm, f + 1)
                if f >= 2:
                    act.wait_ge(yT_ready, f - 1)
                act.activation(c_sb[f % 2], bank[2 * (f % 2)][:, SEQ:2 * SEQ], ACT.Copy).then_inc(c_out, 1)

            conv_upper(4)
            conv_upper(5)
            conv_c(0)
            for i in range(4):
                t, g = i // 2, i % 2
                act.wait_ge(q_tr, i + 1)
                act.activation(qT[0:QK, 4 * g:4 * g + 4, t * P:(t + 1) * P],
                               bank[4 + i][0:QK, :].rearrange("p (h s) -> p h s", s=P), ACT.Copy).then_inc(qT_ready, 1)

            def head_exp(h):
                act.wait_ge(max_ready, h + 1)
                if h >= 2:
                    act.wait_ge(p_tr, h - 1)
                for t in range(TT):
                    c = TT * h + t
                    last = act.activation(prob[h % 2][:, t, :], bank[4 + h % 2][:, t * SEQ:(t + 1) * SEQ], ACT.Exp,
                                          bias=nm[:, c:c + 1], scale=rq[:, c:c + 1], accum_out=sums[:, c:c + 1])
                last.then_inc(exp_ready, 1)

            def head_pair_out(i):
                act.wait_ge(o_mm, 2 * i + 2)
                act.activation(oT[:, i, :], bank[7][:, 0:SEQ], ACT.Copy).then_inc(oT_ready, 1)

            conv_upper(6)
            head_exp(0)
            conv_c(1)
            for h in range(HEADS):
                if 7 + h < 3 * CT:
                    conv_upper(7 + h)
                elif h == 5:
                    gates_upper(0)
                if h + 1 < HEADS:
                    head_exp(h + 1)
                act.wait_ge(p_tr, h + 1)
                act.activation(prob_t[h % 2], bank[6][:, :].rearrange("p (k s) -> p k s", s=SEQ), ACT.Copy).then_inc(pT_ready, 1)
                if h % 2 == 0 and h:
                    head_pair_out(h // 2 - 1)
                if h in (3, 6):
                    conv_c(2 if h == 3 else 3)
                if h == 6:
                    gates_upper(1)
            head_pair_out(HEADS // 2 - 1)

            def branches_upper(d):
                if d == 2:
                    act.wait_ge(mla_in, 16)
                    act.wait_ge(cnv_in, 16)
                if d >= 4:
                    act.wait_ge(y_mm, d - 1)
                upper(branch_up[d % 2], w_branch[:, :, d * P:(d + 1) * P]).then_inc(branch_up_w, 1)

            def gate_sigmoid(d):
                act.wait_ge(gate_mm, d + 1)
                if d >= 2:
                    act.wait_ge(merged, d - 1)
                act.activation(sig[d % 2], bank[2 * (d % 2)][:, :].rearrange("p (g s) -> p g s", s=SEQ), ACT.Sigmoid).then_inc(sig_ready, 1)

            act.wait_ge(o_mm, HEADS)
            act.wait_ge(yT_ready, CT)
            gates_upper(2)
            upper(hT_parts[0], hT).then_inc(hT_up_ready, 1)
            gate_sigmoid(0)
            act.wait_ge(oT_ready, CT)
            upper(ocT_up[:, 0:CT, :], oT)
            upper(ocT_up[:, CT:, :], yT).then_inc(ocT_up_ready, 1)
            gates_upper(3)
            gate_sigmoid(1)
            branches_upper(2)
            for d in range(2, KT):
                gate_sigmoid(d)
                if d + 1 < KT:
                    branches_upper(d + 1)
                if d + 2 < KT:
                    gates_upper(d + 2)
            for i in range(2):
                for t in range(TT):
                    act.wait_ge(x1_ready, 2 * i + t + 1)
                    last = act.activation(h_sb[:, t, 512 * i:512 * i + 512], x_sb[:, t, 512 * i:512 * i + 512], ACT.Square, accum_out=ss[:, 40 + 2 * t + i:41 + 2 * t + i])
                    if i == 1:
                        last.then_inc(x1_sq, 1)
                        act.wait_ge(rs_ready, 6 + t)
                        act.activation(h_sb[:, t, :], x_sb[:, t, :], ACT.Copy, scale=rs[:, 40 + t:41 + t]).then_inc(h2_ready, 1)
            for t in range(TT):
                act.wait_ge(ntop_ready, t + 1)
                act.activation(ew[:, t, :], logit[:, t, :], ACT.Exp, bias=ntop[:, t:t + 1]).then_inc(ew_ready, 1)

            def sigmoid(e):
                act.wait_ge(gate_ready, e + 1)
                act.activation(sg_sb, gate_sb, ACT.Sigmoid, scale=ALPHA).then_inc(esig_ready, 1)

            def expert_out(e, a):
                act.wait_ge(act_tr, e + 1)
                act.activation(actT, ATP[:, :].rearrange("p (j s) -> p j s", s=P), ACT.Copy).then_inc(actT_ready, 1)
                act.wait_ge(w2_used, e * KT + 2 * KT)
                act.activation(y_sb[a * CH:(a + 1) * CH, 1, :], YP[CH:P, :], ACT.Copy).then_inc(y_high, 1)

            def two_experts(j, c, last):
                pair = j + PAIRS * c
                sigmoid(pair * 2 + 1)
                expert_out(pair * 2, 0)
                if not last:
                    sigmoid(pair * 2 + 2)
                act.wait_ge(pickw_tr, pair + 1)
                act.activation(comb, CTP[:, 0:SEQ].rearrange("p (t s) -> p t s", s=P), ACT.Copy).then_inc(comb_ready, 1)
                expert_out(pair * 2 + 1, 1)

            def experts(c):
                sigmoid(c * EXPERTS)
                with act.Fori(0, PAIRS - 1) as j:
                    two_experts(j, c, False)
                two_experts(PAIRS - 1, c, True)

            experts(0)
            act.wait_ge(count_ready, 1)
            most = act.value_load(cmax_i[0:1, 0:1], min_val=0, max_val=SEQ)
            with act.If(most > CH):
                with act.Fori(1, PASSES) as c:
                    with act.If(most > c * CH):
                        experts(c)

        @block.tensor
        def _(pe):
            def warm(n):
                for _ in range(n):
                    pe.matmul(bank[6][:, 0:P], ident[:, :], ident[:, :], start=True, stop=True)

            pe.wait_ge(consts, 1)
            warm(WARM)
            pe.wait_ge(par_in, 80)
            pe.wait_ge(pos_ready, 1)
            pe.transpose(bank[7][:, 0:31], par[0:31, :], ident[0:31, 0:31])
            pe.transpose(bank[7][:, 32:34], pos_f[:, :], ident[0:TT, 0:TT]).then_inc(par_tr, 1)
            warm(WARM // 2)
            for t in range(TT):
                pe.wait_ge(h_ready, t + 1)
                for k in range(KT):
                    last = pe.transpose(bank[2 * t + k // 4][:, (k % 4) * P:(k % 4 + 1) * P], h_sb[:, t, k * P:(k + 1) * P], ident[:, :])
                    if k % 4 == 3:
                        last.then_inc(h_tr, 1)
            for t in range(TT):
                pe.wait_ge(hT_ready, 2 * t + 2)
                for k in range(KT):
                    pe.wait_ge(wa_in[k // 4], 16)
                    last = pe.matmul(bank[4 + 2 * t][:, 0:A_COLS], hT[:, k, t * P:(t + 1) * P], w_a[:, k, :], start=(k == 0), stop=(k == KT - 1))
                last.then_inc(lat_mm, 1)
            for t in range(TT):
                pe.wait_ge(lat_ready, t + 1)
                for k in range(3):
                    last = pe.transpose(bank[5 + 2 * t][:, k * P:(k + 1) * P], lat[:, t, k * P:(k + 1) * P], ident[:, :])
                last.then_inc(lat_tr, 1)
                pe.wait_ge(latT_ready, t + 1)
                pe.wait_ge(uq_in, 16)
                for i in range(2):
                    for k in range(2):
                        last = pe.matmul(bank[2 * t + i][:, 0:4 * QK], latT[:, k, t * P:(t + 1) * P],
                                         w_uq_sb[:, k, i * 4 * QK:(i + 1) * 4 * QK], start=(k == 0), stop=(k == 1))
                last.then_inc(q_mm, 1)
                pe.wait_ge(ukv_in, 16)
                for i in range(2):
                    last = pe.matmul(bank[4 + 2 * t + i][:, :], latT[:, 2, t * P:(t + 1) * P], w_ukv_sb[:, 512 * i:512 * i + 512], start=True, stop=True)
                last.then_inc(kv_mm, 1)

            def in_parts(dst, w, v, first, last):
                for n, (i, j) in enumerate(((0, 1), (1, 0), (0, 0))):
                    ins = pe.matmul(dst, w[i].bitcast(part32), v[j].bitcast(part32), start=(first and n == 0), stop=(last and n == 2))
                return ins

            def conv_group(i):
                f, part = divmod(i, 3)
                pair = 2 * (f % 2)
                if part == 0:
                    if f < 2:
                        pe.wait_ge(q_out, f + 1)
                        pe.wait_ge(q_sq, f + 1)
                    else:
                        pe.wait_ge(yT_ready, f - 1)
                dst = bank[pair + part // 2][:, (part % 2) * SEQ:(part % 2 + 1) * SEQ]
                if i >= WHOLE:
                    pe.wait_ge(conv_low_w, i - WHOLE + 1)
                    pe.wait_ge(hT_low_ready, 1)
                for k in range(KT):
                    if part == 2:
                        cols = slice(f * P, (f + 1) * P)
                        whole, low = w_b[:, k, cols], w_b_low[:, k, cols]
                    else:
                        cols = slice(part * CW + f * P, part * CW + (f + 1) * P)
                        whole, low = w_uc[:, k, cols], w_uc_low[:, k, cols]
                    if i >= WHOLE:
                        last = in_parts(dst, (conv_up[i % 3][:, k, :], low), [v[:, k, :] for v in hT_early], k == 0, k == KT - 1)
                    else:
                        pe.wait_ge(b_in if part == 2 else uc_in[k // 4], 16)
                        last = pe.matmul(dst, whole, hT[:, k, :], start=(k == 0), stop=(k == KT - 1))
                if part == 1:
                    last.then_inc(uc_mm, 1)
                elif part == 2:
                    last.then_inc(b_mm, 1)

            def head_scores(h):
                if h >= 2:
                    pe.wait_ge(exp_ready, h - 1)
                for t in range(TT):
                    last = pe.matmul(bank[4 + h % 2][:, t * SEQ:(t + 1) * SEQ], qT[0:QK, h, t * P:(t + 1) * P], kT[0:QK, h, :], start=True, stop=True)
                last.then_inc(s_mm, 1)

            def head_out(h):
                pe.wait_ge(pT_ready, h + 1)
                if h >= 2 and h % 2 == 0:
                    pe.wait_ge(oT_ready, h // 2)
                for k in range(TT):
                    last = pe.matmul(bank[7][VH * (h % 2):VH * (h % 2) + VH, 0:SEQ], kvx[:, k, h, QK:KVX], prob_t[h % 2][:, k, :], start=(k == 0), stop=(k == TT - 1))
                last.then_inc(o_mm, 1)

            def gates(d):
                if d < 2:
                    pe.wait_ge(yT_ready, d + 3)
                else:
                    pe.wait_ge(sig_ready, d - 1)
                pe.wait_ge(gates_in[d // 2], 32)
                pe.wait_ge(gate_low_w, d + 1)
                if d >= 2:
                    pe.wait_ge(hT_low_ready, 2)
                for g in range(2):
                    dst = bank[2 * (d % 2)][:, g * SEQ:(g + 1) * SEQ]
                    for k in range(KT):
                        cols = slice((d % 2) * P, (d % 2 + 1) * P)
                        last = in_parts(dst, (gates_up_of(d)[:, k, g, :], gates_low[d // 2][:, k, g, cols]), [v[:, k, :] for v in (hT_early if d < 2 else hT_parts)], k == 0, k == KT - 1)
                last.then_inc(gate_mm, 1)

            for i in range(4):
                conv_group(i)
            pe.wait_ge(q_ready, 1)
            pe.wait_ge(k_out, 2)
            pe.wait_ge(v_out, 2)
            for i in range(4):
                t, g = i // 2, i % 2
                for h in range(4):
                    last = pe.transpose(bank[4 + i][0:QK, h * P:(h + 1) * P], q_sb[:, t, 4 * g + h, :], ident[:, :])
                last.then_inc(q_tr, 1)
            conv_group(4)
            pe.wait_ge(k_ready, 1)
            for i in range(4):
                t, g = i // 2, i % 2
                pe.wait_ge(qT_ready, i + 1)
                for h in range(4):
                    last = pe.transpose(bank[4 + i][0:QK, h * P:(h + 1) * P], kvx[:, t, 4 * g + h, 0:QK], ident[:, :])
                last.then_inc(k_tr, 1)
            conv_group(5)
            pe.wait_ge(kT_ready, 4)
            head_scores(0)
            for h in range(HEADS):
                if h + 1 < HEADS:
                    head_scores(h + 1)
                if h < 6:
                    conv_group(6 + h)
                elif h == HEADS - 1:
                    gates(0)
                pe.wait_ge(p_norm, h + 1)
                if h >= 1:
                    pe.wait_ge(pT_ready, h)
                for t in range(TT):
                    for k in range(TT):
                        last = pe.transpose(bank[6][:, k * SEQ + t * P:k * SEQ + (t + 1) * P], prob[h % 2][:, t, k * P:(k + 1) * P], ident[:, :])
                last.then_inc(p_tr, 1)
                if h >= 1:
                    head_out(h - 1)
            head_out(HEADS - 1)

            def branches(d):
                if d >= 2:
                    pe.wait_ge(merged, d - 1)
                pe.wait_ge(oT_ready, CT)
                pe.wait_ge(yT_ready, CT)
                pe.wait_ge(mla_in, 16)
                pe.wait_ge(cnv_in, 16)
                if d >= 2:
                    pe.wait_ge(branch_low_w, d - 1)
                    pe.wait_ge(ocT_low_ready, 1)
                for g, v in enumerate((oT, yT)):
                    dst = bank[2 * (d % 2) + 1][:, g * SEQ:(g + 1) * SEQ]
                    for k in range(CT):
                        n, cols = g * CT + k, slice(d * P, (d + 1) * P)
                        if d < 2:
                            last = pe.matmul(dst, w_branch[:, n, cols], v[:, k, :], start=(k == 0), stop=(k == CT - 1))
                        else:
                            last = in_parts(dst, (branch_up[d % 2][:, n, :], branch_low[:, n, cols]), (ocT_up[:, n, :], ocT_low[g][:, k, :]), k == 0, k == CT - 1)
                        if d == KT - 2 and g == 0 and k == 0:
                            last.then_inc(w1_used[1], KT // 2)
                last.then_inc(y_mm, 1)

            for d in range(KT):
                if d + 1 < KT:
                    gates(d + 1)
                branches(d)

            def bias(s, a):
                pe.matmul((GATE, UP)[s][:, :], sel[a], b1_sb[:, s, :], start=True, stop=True)

            def x1_part(t, i, tiles):
                for k in tiles:
                    pe.wait_ge(wo_in[i], 16)
                    if t == 0 and i == 0:
                        pe.wait_ge(merged, k + 1)
                    last = pe.matmul(bank[4 + 2 * t + i][:, :], mergedT[:, k, t * P:(t + 1) * P], w_o_sb[i][:, k, :], start=(k == 0), stop=(k == KT - 1))
                    if t == 0 and i == 0 and k == 0:
                        last.then_inc(w2_used, KT)
                    if t == 0 and i == 1 and k == 0:
                        last.then_inc(w1_used[1], KT // 4)
                    if k == KT - 1:
                        last.then_inc(x1_mm, 1)

            def x1_transposes(t, i):
                pe.wait_ge(x1_ready, 2 * i + t + 1)
                for k in range(4):
                    last = pe.transpose(bank[2 * t + i][:, k * P:(k + 1) * P], x_sb[:, t, (4 * i + k) * P:(4 * i + k + 1) * P], ident[:, :])
                    if t == 1 and i == 1:
                        if k == 0:
                            last.then_inc(w1_used[0], KT)
                        elif k == 1:
                            last.then_inc(w1_used[1], KT // 4)
                last.then_inc(x1_tr, 1)

            def logits(t):
                for k in range(KT):
                    if t == 1 and k == KT // 2:
                        pe.wait_ge(b1_in, 32)
                        pe.wait_ge(sel_ready, 1)
                        bias(0, 0)
                    pe.wait_ge(x1T_ready, 2 * (k // 4) + t + 1)
                    last = pe.matmul(bank[4 + 2 * t][:, 0:EXPERTS], hT[:, k, t * P:(t + 1) * P], rw_sb[:, k, :], start=(k == 0), stop=(k == KT - 1))
                last.then_inc(logit_mm, 1)

            x1_part(0, 0, range(KT))
            x1_part(1, 0, range(KT))
            x1_part(0, 1, range(KT))
            x1_transposes(0, 0)
            x1_transposes(1, 0)
            x1_part(1, 1, range(KT // 2))
            x1_transposes(0, 1)
            pe.wait_ge(router_in, 16)
            logits(0)
            x1_part(1, 1, range(KT // 2, KT))
            pe.wait_ge(mask_ready, 1)
            pe.matmul(bank[4][:, 0:EXPERTS], before[:, :], mask[:, 0, :], start=True, stop=True).then_inc(rank_mm, 1)
            x1_transposes(1, 1)
            logits(1)
            def gather_tile(t, done=None):
                for k in range(KT):
                    dst = (XTP0, XTP1)[k // 4][:, (k % 4) * P:(k % 4 + 1) * P]
                    last = pe.matmul(dst, h_sb[:, t, k * P:(k + 1) * P], pick[:, t, :], start=(t == 0 and k % 4 == 0), stop=True, skip_group_check=True)
                    if done is not None and k % 4 == 3:
                        last.then_inc(done, 1)

            def gather(count):
                pe.wait_ge(pick_ready, count)
                for k in range(KT):
                    dst = (XTP0, XTP1)[k // 4][:, (k % 4) * P:(k % 4 + 1) * P]
                    for t in range(TT):
                        last = pe.matmul(dst, h_sb[:, t, k * P:(k + 1) * P], pick[:, t, :], start=(t == 0), stop=(t == TT - 1))
                    if k % 4 == 3:
                        last.then_inc(gathered, 1)

            pe.wait_ge(h2_ready, 1)
            pe.wait_ge(pick0_ready, 1)
            gather_tile(0)
            pe.wait_ge(mask_ready, 2)
            pe.matmul(bank[5][:, 0:EXPERTS], ones[:, :], mask[:, 0, :], start=True, stop=False)
            pe.matmul(bank[5][:, 0:EXPERTS], before[:, :], mask[:, 1, :], start=False, stop=True)
            pe.matmul(bank[5][:, EXPERTS:2 * EXPERTS], ones[:, :], mask[:, 0, :], start=True, stop=False)
            pe.matmul(bank[5][:, EXPERTS:2 * EXPERTS], ones[:, :], mask[:, 1, :], start=False, stop=True).then_inc(rank_mm, 1)
            bias(1, 0)

            def gate_up(pair, a, biased=False):
                e = pair * 2 + a
                if not biased:
                    pe.wait_ge(sel_ready, e + 1)
                    bias(0, a)
                    bias(1, a)
                for k in range(KT):
                    if a == 0 and k % (KT // 2) == 0:
                        pe.wait_ge(xT_ready, pair * 2 + (k // (KT // 2) + 1))
                    pe.wait_ge(w1_in[a][k], pair * 16 + 16)
                    for s, dst in enumerate((GATE, UP)):
                        for g in range(2):
                            at = s * FF + g * 512
                            last = pe.matmul(dst[g * CH:(g + 1) * CH, :], xT[:, k, a * CH:(a + 1) * CH], w1_of[a][:, k, at:at + 512], start=False, stop=True, skip_group_check=True)
                    last.then_inc(w1_used[a], 1)

            def expert_y(pair, a):
                e = pair * 2 + a
                pe.wait_ge(act_ready, e + 1)
                for q in range(4):
                    last = pe.transpose(ATP[:, q * P:(q + 1) * P], up_sb[:, q * P:(q + 1) * P], ident[:, :])
                last.then_inc(act_tr, 1)
                if a == 1:
                    pe.wait_ge(y_low, e)
                    pe.wait_ge(y_high, e)
                pe.matmul(YP[:, :], sel[a], b2_sb, start=True, stop=True)
                pe.wait_ge(actT_ready, e + 1)
                for k in range(KT):
                    pe.wait_ge(w2_in[k], e * 16 + 16)
                    g, q = divmod(k, 4)
                    for i in range(2):
                        last = pe.matmul(YP[i * CH:(i + 1) * CH, :], actT[:, q, g * CH:(g + 1) * CH], w2_sb[:, k, 512 * i:512 * i + 512], start=False, stop=True, skip_group_check=True)
                    last.then_inc(w2_used, 1)

            def two_experts(j, c, last):
                pair = j + PAIRS * c
                pe.wait_ge(up_ready, pair * 2 + 1)
                gate_up(pair, 1)
                if not last:
                    gather(pair + 2)
                pe.wait_ge(added, pair * 4 + 4)
                expert_y(pair, 0)
                if not last:
                    pe.wait_ge(up_ready, pair * 2 + 2)
                    gate_up(pair + 1, 0)
                pe.wait_ge(pickw_ready, pair + 1)
                for t in range(TT):
                    ins = pe.transpose(CTP[:, t * P:(t + 1) * P], pick_w[:, t, :], ident[:, :])
                ins.then_inc(pickw_tr, 1)
                expert_y(pair, 1)
                pe.wait_ge(comb_ready, pair + 1)
                pe.wait_ge(y_low, pair * 2 + 2)
                pe.wait_ge(y_high, pair * 2 + 2)
                for t, dsts in enumerate(((CMB, CTP), (ATP, YP))):
                    for i in range(2):
                        pe.matmul(dsts[i][:, :], comb[:, t, :], y_sb[:, i, :], start=True, stop=True).then_inc(comb_mm, 1)

            def experts(c):
                pair = c * PAIRS
                if isinstance(c, int):
                    pe.wait_ge(h2_ready, TT)
                    pe.wait_ge(pick_ready, 1)
                    gather_tile(1, gathered)
                    pe.wait_ge(b2_in, 32)
                else:
                    pe.wait_ge(xT_ready, pair * 2)
                    gather(pair + 1)
                    pe.wait_ge(up_ready, pair * 2)
                gate_up(pair, 0, biased=isinstance(c, int))
                with pe.Fori(0, PAIRS - 1) as j:
                    two_experts(j, c, False)
                two_experts(PAIRS - 1, c, True)

            experts(0)
            pe.wait_ge(count_ready, 1)
            most = pe.value_load(cmax_i[0:1, 0:1], min_val=0, max_val=SEQ)
            with pe.If(most > CH):
                with pe.Fori(1, PASSES) as c:
                    with pe.If(most > c * CH):
                        experts(c)

        @block.vector
        def _(dve):
            n_step = [0]

            def link(ins):
                n_step[0] += 1
                ins.then_inc(dve_step, 1)
                dve.wait_ge(dve_step, n_step[0])

            def bc(ap, *shape):
                return ap.to_broadcast(list(shape))

            mult, add, sub = ALU.mult, ALU.add, ALU.subtract
            dve.wait_ge(pos_in, 16)
            dve.tensor_copy(pos_f[:, :], pos_i[:, :]).then_inc(pos_ready, 1)

            def scaled(col, width, size, last=True):
                i = dve.tensor_scalar(ms[:, col:col + width], ss[:, col:col + width], 1.0 / size, EPS, mult, add)
                if last:
                    i.then_inc(ms_ready, 1)

            for t in range(TT):
                dve.wait_ge(x_sq, t + 1)
                scaled(t, 1, D)
            dve.wait_ge(par_tr, 1)
            dve.tensor_copy(parT[:, 0:31], bank[7][:, 0:31])
            link(dve.tensor_copy(parT[:, 32:34], bank[7][:, 32:34]))
            for t in range(TT):
                dve.wait_ge(rs_ready, t + 1)
                dve.tensor_scalar(h_sb[:, t, :], x_sb[:, t, :], rs[:, t:t + 1], None, mult).then_inc(h_ready, 1)

            def norm_out(t, i, g, done):
                dve.tensor_tensor(hT[:, 4 * i:4 * i + 4, t * P:(t + 1) * P], bank[2 * t + i][:, :].rearrange("p (k s) -> p k s", s=P),
                                  bc(parT[:, g + 4 * i:g + 4 * i + 4].unsqueeze(2), P, 4, P), mult).then_inc(done, 1)

            for t in range(TT):
                for i in range(2):
                    dve.wait_ge(h_tr, 2 * t + i + 1)
                    norm_out(t, i, G1, hT_ready)

            def lower(low, whole, up):
                return dve.tensor_tensor(low.bitcast(part32), whole, up, sub)

            def gates_lower(d):
                dve.wait_ge(gate_up_w, d + 1)
                lower(*(w[d // 2][:, :, :, (d % 2) * P:(d % 2 + 1) * P] for w in (gates_low, w_gates)), gates_up_of(d)).then_inc(gate_low_w, 1)

            def conv_lower(i):
                f, part = divmod(i, 3)
                dve.wait_ge(conv_up_w, i - WHOLE + 1)
                if part == 2:
                    pair = [w[:, :, f * P:(f + 1) * P] for w in (w_b_low, w_b)]
                else:
                    pair = [w[:, :, part * CW + f * P:part * CW + (f + 1) * P] for w in (w_uc_low, w_uc)]
                lower(*pair, conv_up[i % 3]).then_inc(conv_low_w, 1)

            dve.wait_ge(consts, 2)
            ang, kk, r, z, sp_, cp_, sn_, cs_ = rope_t
            for t in range(TT):
                last = dve.tensor_scalar(ang[:, t, :], invf[:, :], parT[:, 32 + t:33 + t], None, mult)
            link(last)
            two_pi = 2 * np.pi
            c1 = 6.28125
            c2 = float(np.round((two_pi - c1) * 2 ** 17) / 2 ** 17)
            c3 = two_pi - c1 - c2
            magic = 1.5 * 2 ** 23
            link(dve.tensor_scalar(kk, ang, 1 / two_pi, magic, mult, add))
            link(dve.tensor_scalar(kk, kk, -magic, None, add))
            link(dve.scalar_tensor_tensor(r, kk, -c1, ang, mult, add))
            link(dve.scalar_tensor_tensor(r, kk, -c2, r, mult, add))
            link(dve.scalar_tensor_tensor(r, kk, -c3, r, mult, add))
            link(dve.tensor_scalar(r, r, 0.5, None, mult))
            link(dve.tensor_tensor(z, r, r, mult))
            s_c, c_c, f = [], [], 1.0
            for i in range(1, 14):
                f *= i
                (s_c if i % 2 else c_c).append((-1) ** (i // 2) / f)
            s_c = s_c[1:]
            dve.tensor_scalar(sp_, z, s_c[-1], None, mult)
            link(dve.tensor_scalar(cp_, z, c_c[-1], None, mult))
            for i in range(len(s_c) - 2, -1, -1):
                dve.scalar_tensor_tensor(sp_, sp_, s_c[i], z, add, mult)
                link(dve.scalar_tensor_tensor(cp_, cp_, c_c[i], z, add, mult))
            dve.scalar_tensor_tensor(sn_, sp_, 1.0, r, add, mult)
            link(dve.tensor_scalar(cs_, cp_, 1.0, None, add))
            cos_t, sin_t = (v[:, :].rearrange("p (t r) -> p t r", t=TT) for v in (cos_sb, sin_sb))
            dve.scalar_tensor_tensor(sin_t, sn_, 2.0, cs_, mult, mult)
            link(dve.scalar_tensor_tensor(cos_t, sn_, -2.0, sn_, mult, mult))
            link(dve.tensor_scalar(cos_t, cos_t, 1.0, None, add))

            dve.wait_ge(hT_up_ready, 1)
            lower(hT_early[1], hT, hT_early[0]).then_inc(hT_low_ready, 1)
            dve.wait_ge(gains_in, 32)
            for t in range(TT):
                raw = bank[4 + 2 * t]
                dve.wait_ge(lat_sq, t + 1)
                scaled(2 + 2 * t, 1, QL, last=False)
                scaled(3 + 2 * t, 1, KVL)
                dve.tensor_tensor(krg[:, t, :], raw[:, QL + KVL:A_COLS], kg_sb[:, NOPE:QK], mult)
                dve.wait_ge(rs_ready, 3 + t)
                dve.tensor_scalar(lat[:, t, 0:QL], raw[:, 0:QL], rs[:, 2 + 2 * t:3 + 2 * t], None, mult)
                dve.tensor_scalar(lat[:, t, QL:], raw[:, QL:QL + KVL], rs[:, 3 + 2 * t:4 + 2 * t], None, mult).then_inc(lat_ready, 1)
                dve.wait_ge(lat_tr, t + 1)
                dve.tensor_tensor(latT[:, :, t * P:(t + 1) * P], bank[5 + 2 * t][:, 0:3 * P].rearrange("p (k s) -> p k s", s=P),
                                  bc(parT[:, GL:GL + 3].unsqueeze(2), P, 3, P), mult).then_inc(latT_ready, 1)

            def rotate(src, tmp, dst, cos, sin, shape):
                t1, t2 = src(0), src(1)
                dve.tensor_tensor(tmp[0], t1, cos, mult)
                dve.tensor_tensor(tmp[1], t2, sin, mult)
                dve.tensor_tensor(tmp[2], t1, sin, mult)
                link(dve.tensor_tensor(tmp[3], t2, cos, mult))
                dve.tensor_tensor(dst(0), tmp[0], tmp[1], sub)
                return dve.tensor_tensor(dst(1), tmp[2], tmp[3], add)

            link(rotate(lambda i: krg[:, :, i * HR:(i + 1) * HR], krot_tmp,
                        lambda i: krot[:, :].rearrange("p (t r) -> p t r", t=TT)[:, :, i * HR:(i + 1) * HR],
                        cos_t, sin_t, None))
            for t in range(TT):
                dve.wait_ge(q_sq, t + 1)
                for i in range(2):
                    last = dve.tensor_tensor(q_sb[:, t, 4 * i:4 * i + 4, :], bank[2 * t + i][:, 0:4 * QK].rearrange("p (h d) -> p h d", d=QK),
                                             bc(qg_sb[:, :].unsqueeze(1), P, 4, QK), mult)
                last.then_inc(q_out, 1)
            for t in range(TT):
                dve.tensor_reduce(ss[:, 8 + 8 * t:16 + 8 * t], sq_q[t], AX.X, add)
            for t in range(TT):
                dve.wait_ge(v_out, t + 1)
                for i in range(2):
                    kv = bank[4 + 2 * t + i][:, :].rearrange("p (h d) -> p h d", d=NOPE + VH)
                    last = dve.tensor_tensor(kvx[:, t, 4 * i:4 * i + 4, 0:NOPE], kv[:, :, 0:NOPE],
                                             bc(kg_sb[:, 0:NOPE].unsqueeze(1), P, 4, NOPE), mult)
                last.then_inc(k_out, 1)
            for t in range(TT):
                last = dve.tensor_reduce(ss[:, 24 + 8 * t:32 + 8 * t], sq_k[t], AX.X, add)
            link(last)
            for t in range(TT):
                last = dve.tensor_scalar(ss[:, 24 + 8 * t:32 + 8 * t], ss[:, 24 + 8 * t:32 + 8 * t], ss[:, 6 + t:7 + t], None, add)
            link(last)
            scaled(8, 32, QK)
            wide = [bc(v.unsqueeze(2), P, TT, HEADS, HR) for v in (cos_t, sin_t)]
            half = lambda i: q_sb[:, :, :, NOPE + i * HR:NOPE + (i + 1) * HR]
            dve.wait_ge(q_out, 2)
            rotate(half, rot_tmp, half, wide[0], wide[1], None).then_inc(q_ready, 1)
            dve.wait_ge(rs_ready, 5)
            dve.wait_ge(k_out, 2)
            for t in range(TT):
                rk = rs[:, 24 + 8 * t:32 + 8 * t].unsqueeze(2)
                dve.tensor_tensor(kvx[:, t, :, 0:NOPE], kvx[:, t, :, 0:NOPE], bc(rk, P, HEADS, NOPE), mult)
                last = dve.tensor_tensor(kvx[:, t, :, NOPE:QK], bc(krot[:, t * ROPE:(t + 1) * ROPE].unsqueeze(1), P, HEADS, ROPE),
                                         bc(rk, P, HEADS, ROPE), mult)
            last.then_inc(k_ready, 1)
            link(dve.tensor_scalar(rq[:, :].rearrange("p (h t) -> p t h", t=TT), rs[:, 8:24].rearrange("p (t h) -> p t h", t=TT),
                                   float(QK) ** -0.5, None, mult))

            def conv(f):
                u, b = bank[2 * (f % 2)][:, 0:SEQ], bank[2 * (f % 2) + 1][:, 0:SEQ]
                c, y = cu[f % 2], y_tmp[f % 2]
                w = [parT[:, GC + CT * i + f:GC + CT * i + f + 1] for i in range(3)]
                if f < 2:
                    dve.memset(c[:, 0:1], 0.0)
                    dve.memset(c[:, SEQ + 1:SEQ + 2], 0.0)
                dve.wait_ge(c_out, f + 1)
                link(dve.tensor_tensor(c[:, 1:SEQ + 1], u, c_sb[f % 2], mult))
                link(dve.tensor_scalar(y, c[:, 0:SEQ], w[0], None, mult))
                link(dve.scalar_tensor_tensor(y, c[:, 1:SEQ + 1], w[1], y, mult, add))
                link(dve.scalar_tensor_tensor(y, c[:, 2:SEQ + 2], w[2], y, mult, add))
                dve.wait_ge(b_mm, f + 1)
                dve.tensor_tensor(yT[:, f, :], b, y, mult).then_inc(yT_ready, 1)

            def head_max(h):
                dve.wait_ge(s_mm, h + 1)
                pair = slice(TT * h, TT * h + TT)
                link(dve.tensor_reduce(mx[:, pair], bank[4 + h % 2][:, :].rearrange("p (t s) -> p t s", t=TT), AX.X, ALU.max))
                dve.scalar_tensor_tensor(nm[:, pair], mx[:, pair], -1.0, rq[:, pair], mult, mult).then_inc(max_ready, 1)

            def head_norm(h):
                dve.wait_ge(exp_ready, h + 1)
                pair = slice(TT * h, TT * h + TT)
                link(dve.reciprocal(rsum[:, pair], sums[:, pair]))
                for t in range(TT):
                    last = dve.tensor_scalar(prob[h % 2][:, t, :], prob[h % 2][:, t, :], rsum[:, TT * h + t:TT * h + t + 1], None, mult)
                last.then_inc(p_norm, 1)

            conv_lower(4)
            conv_lower(5)
            conv(0)
            for i in range(4):
                t, g = i // 2, i % 2
                dve.wait_ge(k_tr, i + 1)
                dve.tensor_copy(kT[0:QK, 4 * g:4 * g + 4, t * P:(t + 1) * P], bank[4 + i][0:QK, :].rearrange("p (h s) -> p h s", s=P)).then_inc(kT_ready, 1)
            conv_lower(6)
            head_max(0)
            head_norm(0)
            for h in range(HEADS):
                if h + 1 < HEADS:
                    head_max(h + 1)
                    if 7 + h < 3 * CT:
                        conv_lower(7 + h)
                    elif h == 5:
                        gates_lower(0)
                    head_norm(h + 1)
                if h in (0, 3, 6):
                    conv(1 + h // 3)
            gates_lower(1)

            def branches_lower(d):
                dve.wait_ge(branch_up_w, d - 1)
                lower(*(w[:, :, d * P:(d + 1) * P] for w in (branch_low, w_branch)), branch_up[d % 2]).then_inc(branch_low_w, 1)

            def merge(d):
                dve.wait_ge(sig_ready, d + 1)
                dve.wait_ge(y_mm, d + 1)
                g = gated[d % 2]
                link(dve.tensor_tensor(g, sig[d % 2], bank[2 * (d % 2) + 1][:, :].rearrange("p (g s) -> p g s", s=SEQ), mult))
                dve.tensor_tensor(mergedT[:, d, :], g[:, 0, :], g[:, 1, :], add).then_inc(merged, 1)

            gates_lower(2)
            dve.wait_ge(hT_up_ready, 2)
            dve.wait_ge(gate_mm, 2)
            lower(hT_parts[1], hT, hT_parts[0]).then_inc(hT_low_ready, 1)
            merge(0)
            gates_lower(3)
            branches_lower(2)
            merge(1)
            dve.wait_ge(ocT_up_ready, 1)
            lower(ocT_low[0], oT, ocT_up[:, 0:CT, :])
            lower(ocT_low[1], yT, ocT_up[:, CT:, :]).then_inc(ocT_low_ready, 1)
            for d in range(2, KT):
                if d + 2 < KT:
                    gates_lower(d + 2)
                if d + 1 < KT:
                    branches_lower(d + 1)
                merge(d)
            def x1_add(t, i):
                dve.wait_ge(x1_mm, 2 * i + t + 1)
                cols = slice(512 * i, 512 * i + 512)
                dve.tensor_tensor(x_sb[:, t, cols], bank[4 + 2 * t + i][:, :], x_sb[:, t, cols], add).then_inc(x1_ready, 1)

            def x1T_out(t, i):
                dve.wait_ge(x1_tr, 2 * i + t + 1)
                norm_out(t, i, G2, x1T_ready)

            def x1_norm(t):
                dve.wait_ge(x1_sq, t + 1)
                link(dve.tensor_tensor(ss[:, 40 + 2 * t:41 + 2 * t], ss[:, 40 + 2 * t:41 + 2 * t], ss[:, 41 + 2 * t:42 + 2 * t], add))
                dve.tensor_scalar(ms[:, 40 + t:41 + t], ss[:, 40 + 2 * t:41 + 2 * t], 1.0 / D, EPS, mult, add).then_inc(ms_ready, 1)

            def route(t):
                eight = slice(8 * t, 8 * t + 8)
                dve.wait_ge(rs_ready, 6 + t)
                dve.wait_ge(logit_mm, t + 1)
                link(dve.scalar_tensor_tensor(logit[:, t, :], bank[4 + 2 * t][:, 0:EXPERTS], rs[:, 40 + t:41 + t], rb_sb[:, :], mult, add))
                link(dve.max(top[:, eight], logit[:, t, :]))
                link(dve.max_index(topi[:, eight], top[:, eight], logit[:, t, :]))
                link(dve.tensor_tensor(first4, expert_no[:, :].rearrange("p (j e) -> p j e", j=TOPK),
                                       bc(topi[:, 8 * t:8 * t + TOPK].unsqueeze(2), P, TOPK, EXPERTS), ALU.is_equal))
                dve.tensor_reduce(mask[:, t, :], first4.rearrange("p j e -> p e j"), AX.X, add).then_inc(mask_ready, 1)
                dve.tensor_scalar(ntop[:, t:t + 1], top[:, 8 * t:8 * t + 1], -1.0, None, mult).then_inc(ntop_ready, 1)

            def first_selectors():
                for a in range(2):
                    dve.tensor_scalar(sel[a], half_mask, one_hot[:, a:a + 1], None, mult).then_inc(sel_ready, 1)

            def get_rank(t):
                dve.wait_ge(mask_ready, t + 1)
                dve.wait_ge(rank_mm, t + 1)
                link(dve.scalar_tensor_tensor(rank[:, t, 0:EXPERTS], bank[4 + t][:, 0:EXPERTS], 1.0, mask[:, t, :], add, mult))

            def build_pick(cols, tiles=range(TT), done=pick_ready):
                for t in tiles:
                    for a in range(2):
                        last = dve.tensor_scalar(pick[:, t, a * CH:(a + 1) * CH], slots[:, :], rank[:, t, cols[a]], None, ALU.is_equal)
                last.then_inc(done, 1)

            dve.wait_ge(consts2, 1)
            first_selectors()
            dve.wait_ge(rb_in, 16)
            x1_add(0, 0)
            x1_add(1, 0)
            x1_add(0, 1)
            x1T_out(0, 0)
            x1T_out(1, 0)
            x1_norm(0)
            x1T_out(0, 1)
            route(0)
            x1_add(1, 1)
            get_rank(0)
            build_pick([slice(0, 1), slice(1, 2)], [0], pick0_ready)
            x1T_out(1, 1)
            x1_norm(1)
            route(1)
            get_rank(1)
            def gather_out(count):
                for i, src in enumerate((XTP0, XTP1)):
                    dve.wait_ge(gathered, count * 2 + (i - 1))
                    dve.tensor_tensor(xT[:, 4 * i:4 * i + 4, :], src[:, :].rearrange("p (k s) -> p k s", s=P),
                                      bc(parT[:, G2 + 4 * i:G2 + 4 * i + 4].unsqueeze(2), P, 4, P), mult).then_inc(xT_ready, 1)

            def swiglu(pair, a, first=False):
                e = pair * 2 + a
                dve.wait_ge(w1_used[a], pair * KT + 2 * KT)
                dve.tensor_scalar(gate_sb, GATE[:, :], LIMIT, None, ALU.min).then_inc(gate_ready, 1)
                if not first:
                    dve.wait_ge(act_tr, e)
                dve.tensor_scalar(up_sb, UP[:, :], LIMIT, -LIMIT, ALU.min, ALU.max).then_inc(up_ready, 1)
                dve.wait_ge(up_ready, e + 1)
                dve.scalar_tensor_tensor(up_sb, up_sb, 1.0, gate_sb, add, mult).then_inc(prod_ready, 1)
                dve.wait_ge(prod_ready, e + 1)
                dve.wait_ge(esig_ready, e + 1)
                dve.tensor_tensor(up_sb, up_sb, sg_sb, mult).then_inc(act_ready, 1)

            def output_half(pair, a, next_col):
                used = pair * (2 * KT) + (a * KT + KT)
                if next_col is not None:
                    dve.wait_ge(w2_used, used + 1)
                    dve.tensor_scalar(sel[a], half_mask, one_hot[:, next_col], None, mult).then_inc(sel_ready, 1)
                dve.wait_ge(w2_used, used + KT)
                dve.tensor_copy(y_sb[a * CH:(a + 1) * CH, 0, :], YP[0:CH, :]).then_inc(y_low, 1)

            def two_experts(j, c, last):
                pair = j + PAIRS * c
                if not last:
                    build_pick([ds(j * 2 + 2, 1), ds(j * 2 + 3, 1)])
                for t in range(TT):
                    for a in range(2):
                        ins = dve.tensor_scalar(pick_w[:, t, a * CH:(a + 1) * CH], slots[:, :], rank[:, t, ds(j * 2 + a, 1)], wd[:, t, ds(j * 2 + a, 1)], ALU.is_equal, mult)
                ins.then_inc(pickw_ready, 1)
                swiglu(pair, 1)
                if not last:
                    gather_out(pair + 2)
                output_half(pair, 0, None if last else ds(j * 2 + 2, 1))
                if not last:
                    swiglu(pair + 1, 0)
                output_half(pair, 1, None if last else ds(j * 2 + 3, 1))
                for t, dsts in enumerate(((CMB, CTP), (ATP, YP))):
                    for i in range(2):
                        dve.wait_ge(comb_mm, pair * 4 + (2 * t + i + 1))
                        cols = slice(512 * i, 512 * i + 512)
                        dve.tensor_tensor(x_sb[:, t, cols], dsts[i][:, :], x_sb[:, t, cols], add).then_inc(added, 1)

            def experts(c):
                if not isinstance(c, int):
                    dve.tensor_scalar(rank[:, :, :], rank[:, :, :], -float(CH), None, add).then_inc(rank_moved, 1)
                    dve.wait_ge(rank_moved, c)
                if isinstance(c, int):
                    build_pick([slice(0, 1), slice(1, 2)], [1])
                else:
                    build_pick([slice(0, 1), slice(1, 2)])
                    first_selectors()
                if isinstance(c, int):
                    link(dve.tensor_reduce(cmax[:, :], bank[5][:, EXPERTS:2 * EXPERTS], AX.X, ALU.max))
                    dve.tensor_copy(cmax_i[:, :], cmax[:, :]).then_inc(count_ready, 1)
                gather_out(c * PAIRS + 1)
                if isinstance(c, int):
                    for t in range(TT):
                        dve.wait_ge(ew_ready, t + 1)
                        last = dve.scalar_tensor_tensor(ew[:, t, :], ew[:, t, :], 1.0, mask[:, t, :], mult, mult, accum_out=esum[:, t:t + 1])
                    link(last)
                    link(dve.reciprocal(ersum[:, :], esum[:, :]))
                    for t in range(TT):
                        last = dve.tensor_scalar(wd[:, t, :], ew[:, t, :], ersum[:, t:t + 1], None, mult)
                    last.then_inc(added, 2 * TT)
                    dve.wait_ge(added, 2 * TT)
                swiglu(c * PAIRS, 0, first=isinstance(c, int))
                with dve.Fori(0, PAIRS - 1) as j:
                    two_experts(j, c, False)
                two_experts(PAIRS - 1, c, True)

            experts(0)
            dve.wait_ge(count_ready, 1)
            most = dve.value_load(cmax_i[0:1, 0:1], min_val=0, max_val=SEQ)
            with dve.If(most > CH):
                with dve.Fori(1, PASSES) as c:
                    with dve.If(most > c * CH):
                        experts(c)


_INS = ['x', 'positions', 'norm1_g', 'w_in', 'q_a_norm_g', 'kv_a_norm_g', 'w_uq', 'w_ukv', 'q_norm_g', 'k_norm_g',
        'conv_w', 'w_o_mla', 'w_o_conv', 'w_o', 'norm2_g', 'router_w', 'router_b', 'expert_w1', 'expert_b1',
        'expert_w2', 'expert_b2']


def kernel(**inputs):
    import numpy as _np
    import concourse.bacc as _bacc
    from concourse import mybir as _mybir
    from concourse.bass_utils import run_bass_kernel_spmd as _run

    nc = _bacc.Bacc("TRN2", target_bir_lowering=False, num_devices=1)
    arrays, args = {}, []
    for name in _INS:
        a = _np.ascontiguousarray(inputs[name])
        arrays[f"in_{name}"] = a
        args.append(nc.dram_tensor(f"in_{name}", a.shape, _mybir.dt.from_np(a.dtype), kind="ExternalInput").ap())
    args.append(nc.dram_tensor("out_x", (1, SEQ, D), _mybir.dt.float32, kind="ExternalOutput").ap())
    build(nc, *args)
    r = _run(nc, [arrays], core_ids=[0])
    return r.results[0]["out_x"]
```
